# Optimizing a Trainium2 kernel written in Bass

```python
import math
import jax, jax.numpy as jnp
from jax import lax
import numpy as np

D_MODEL = 1024
BATCH = 1
SEQ = 512
DEPTH = 2

N_MIXERS = 2
HEAD_DIM = 64
FOX_HEADS = D_MODEL // HEAD_DIM
DIL_GROUPS = ((128, 1), (512, 4), (2048, 16))
N_GROUPS = len(DIL_GROUPS)
DIL_HEADS = D_MODEL // HEAD_DIM
ROT_DIM = HEAD_DIM // 4
ROPE_THETA = 500000.0
D_FF = 4 * D_MODEL
Q_BLOCK = 128
EPS = 1e-6
NEG_INF = -1e30
N_FOX_LAYERS = (DEPTH + 1) // 2
N_DIL_LAYERS = DEPTH // 2

kernel_name = "fox_dilated_hybrid_trunk"

def _rmsnorm(x, g):
    xf = x.astype(jnp.float32)
    y = xf * lax.rsqrt(jnp.mean(xf * xf, axis=-1, keepdims=True) + EPS)
    return (y * g.astype(jnp.float32)).astype(x.dtype)

def _partial_rope(x, positions):
    half = ROT_DIM // 2
    inv = ROPE_THETA ** (-jnp.arange(half, dtype=jnp.float32) * 2.0 / ROT_DIM)
    ang = positions.astype(jnp.float32)[:, :, None] * inv
    cos = jnp.cos(ang)[:, :, None, :]
    sin = jnp.sin(ang)[:, :, None, :]
    xf = x.astype(jnp.float32)
    x1 = xf[..., :half]
    x2 = xf[..., half:ROT_DIM]
    out = jnp.concatenate([x1 * cos - x2 * sin, x2 * cos + x1 * sin, xf[..., ROT_DIM:]], axis=-1)
    return out.astype(x.dtype)

def _fox_attention(h, w_in, b_f, q_gain, k_gain, w_out):
    B, S, _ = h.shape
    H, Dh = FOX_HEADS, HEAD_DIM
    proj = h @ w_in
    q = _rmsnorm(proj[..., :H * Dh].reshape(B, S, H, Dh), q_gain)
    k = _rmsnorm(proj[..., H * Dh:2 * H * Dh].reshape(B, S, H, Dh), k_gain)
    v = proj[..., 2 * H * Dh:3 * H * Dh].reshape(B, S, H, Dh)
    log_f = jax.nn.log_sigmoid((proj[..., 3 * H * Dh:] + b_f).astype(jnp.float32))
    c = jnp.cumsum(log_f, axis=1).transpose(0, 2, 1)
    scale = 1.0 / math.sqrt(Dh)
    outs = []
    for i in range(S // Q_BLOCK):
        lo, hi = i * Q_BLOCK, (i + 1) * Q_BLOCK
        s = jnp.einsum('bqhd,bkhd->bhqk', q[:, lo:hi], k[:, :hi]).astype(jnp.float32) * scale
        s = s + (c[:, :, lo:hi, None] - c[:, :, None, :hi])
        causal = jnp.arange(hi)[None, :] <= jnp.arange(lo, hi)[:, None]
        s = jnp.where(causal, s, NEG_INF)
        p = jax.nn.softmax(s, axis=-1)
        outs.append(jnp.einsum('bhqk,bkhd->bqhd', p.astype(v.dtype), v[:, :hi]))
    o = jnp.concatenate(outs, axis=1).reshape(B, S, H * Dh)
    return o @ w_out

def _dilated_group(q, k, v, window, dilation):
    B, S, H, Dh = q.shape
    d = dilation
    L = S // d
    n = window // d
    blk = n
    nb = -(-L // blk)
    Lp = nb * blk

    def to_sub(t):
        t = t.reshape(B, L, d, H, Dh).transpose(0, 2, 1, 3, 4)
        t = jnp.pad(t, ((0, 0), (0, 0), (0, Lp - L), (0, 0), (0, 0)))
        return t.reshape(B, d, nb, blk, H, Dh)

    def with_prev(t):
        prev = jnp.pad(t[:, :, :-1], ((0, 0), (0, 0), (1, 0), (0, 0), (0, 0), (0, 0)))
        return jnp.concatenate([prev, t], axis=3)

    qs = to_sub(q)
    kk = with_prev(to_sub(k))
    vv = with_prev(to_sub(v))
    scale = 1.0 / math.sqrt(Dh)
    s = jnp.einsum('brnqhe,brnkhe->brnhqk', qs, kk).astype(jnp.float32) * scale
    qi = jnp.arange(blk)[:, None]
    kj = jnp.arange(2 * blk)[None, :]
    dist = qi + blk - kj
    band = (dist >= 0) & (dist <= n)
    has_prev = (jnp.arange(nb)[:, None, None] > 0) | (kj[None] >= blk)
    mask = band[None] & has_prev
    s = jnp.where(mask[None, None, :, None], s, NEG_INF)
    m = jnp.max(s, axis=-1, keepdims=True)
    p = jnp.exp(s - m)
    den = jnp.sum(p, axis=-1, keepdims=True)
    o = jnp.einsum('brnhqk,brnkhe->brnqhe', (p / den).astype(vv.dtype), vv)
    lse = (m + jnp.log(den))[..., 0]
    o = o.reshape(B, d, Lp, H, Dh)[:, :, :L].transpose(0, 2, 1, 3, 4).reshape(B, S, H, Dh)
    lse = lse.transpose(0, 1, 2, 4, 3).reshape(B, d, Lp, H)[:, :, :L]
    lse = lse.transpose(0, 2, 1, 3).reshape(B, S, H)
    return o, lse

def _dilated_attention(h, positions, w_in, q_gain, k_gain, w_out):
    B, S, _ = h.shape
    H, Dh = DIL_HEADS, HEAD_DIM
    proj = (h @ w_in).reshape(B, S, N_GROUPS, 3, H, Dh)
    outs, lses = [], []
    for g, (window, dil) in enumerate(DIL_GROUPS):
        q = _partial_rope(_rmsnorm(proj[:, :, g, 0], q_gain[g]), positions)
        k = _partial_rope(_rmsnorm(proj[:, :, g, 1], k_gain[g]), positions)
        o, lse = _dilated_group(q, k, proj[:, :, g, 2], window, dil)
        outs.append(o)
        lses.append(lse)
    wts = jax.nn.softmax(jnp.stack(lses, axis=0), axis=0)
    o = jnp.einsum('gbsh,gbshe->bshe', wts, jnp.stack(outs, axis=0).astype(jnp.float32))
    return o.astype(h.dtype).reshape(B, S, H * Dh) @ w_out

def _sqrelu_mlp(h, w1, w2):
    return jnp.square(jax.nn.relu(h @ w1)) @ w2

def setup_inputs(seed: int = 0) -> dict:
    key = jax.random.key(seed)
    ks = jax.random.split(key, 16)
    D, Dh = D_MODEL, HEAD_DIM
    nA, nB = N_FOX_LAYERS, N_DIL_LAYERS
    nrm = lambda k, shape, fan: jax.random.normal(k, shape, jnp.float32) * fan ** -0.5
    gain = lambda k, shape: 1.0 + 0.02 * jax.random.normal(k, shape, jnp.float32)
    x = jax.random.normal(ks[0], (BATCH, SEQ, D), jnp.float32)
    offset = jax.random.randint(ks[1], (BATCH, 1), 0, 4096, dtype=jnp.int32)
    positions = offset + jnp.arange(SEQ, dtype=jnp.int32)[None, :]
    return {
        "x": x,
        "positions": positions,
        "fox_norm": gain(ks[2], (nA, D)),
        "fox_w_in": nrm(ks[3], (nA, D, 3 * FOX_HEADS * Dh + FOX_HEADS), D),
        "fox_b_f": jax.random.uniform(ks[4], (nA, FOX_HEADS), jnp.float32, 1.0, 5.0),
        "fox_q_gain": gain(ks[5], (nA, Dh)),
        "fox_k_gain": gain(ks[6], (nA, Dh)),
        "fox_w_out": nrm(ks[7], (nA, FOX_HEADS * Dh, D), FOX_HEADS * Dh),
        "dil_norm": gain(ks[8], (nB, D)),
        "dil_w_in": nrm(ks[9], (nB, D, N_GROUPS * 3 * DIL_HEADS * Dh), D),
        "dil_q_gain": gain(ks[10], (nB, N_GROUPS, Dh)),
        "dil_k_gain": gain(ks[11], (nB, N_GROUPS, Dh)),
        "dil_w_out": nrm(ks[12], (nB, DIL_HEADS * Dh, D), DIL_HEADS * Dh),
        "mlp_norm": gain(ks[13], (DEPTH, D)),
        "mlp_w1": nrm(ks[14], (DEPTH, D, D_FF), D),
        "mlp_w2": nrm(ks[15], (DEPTH, D_FF, D), D_FF),
    }

def reference(x, positions, fox_norm, fox_w_in, fox_b_f, fox_q_gain, fox_k_gain, fox_w_out,
              dil_norm, dil_w_in, dil_q_gain, dil_k_gain, dil_w_out,
              mlp_norm, mlp_w1, mlp_w2):
    for i in range(DEPTH):
        j = i // N_MIXERS
        if i % N_MIXERS == 0:
            h = _rmsnorm(x, fox_norm[j])
            x = x + _fox_attention(h, fox_w_in[j], fox_b_f[j], fox_q_gain[j], fox_k_gain[j], fox_w_out[j])
        else:
            h = _rmsnorm(x, dil_norm[j])
            x = x + _dilated_attention(h, positions, dil_w_in[j], dil_q_gain[j], dil_k_gain[j], dil_w_out[j])
        x = x + _sqrelu_mlp(_rmsnorm(x, mlp_norm[i]), mlp_w1[i], mlp_w2[i])
    return x


_drawn_inputs = setup_inputs


def setup_inputs(seed=0):
    import zlib

    import numpy as np

    out = dict(_drawn_inputs(seed))
    spreads = {}
    factors = {'fox_norm': 4.741,
     'fox_q_gain': 8.0,
     'fox_k_gain': 8.0,
     'dil_norm': 8.0,
     'dil_q_gain': 8.0,
     'dil_k_gain': 8.0}
    for name, (base, spread) in spreads.items():
        noise = np.random.default_rng([zlib.crc32(name.encode()), seed]).standard_normal(out[name].shape)
        drawn = base * np.exp(spread * noise) if base else spread * noise
        out[name] = __import__('jax').numpy.asarray(drawn.astype(out[name].dtype))
    for name, factor in factors.items():
        out[name] = (out[name] * factor).astype(out[name].dtype)
    return out
```

```python
from contextlib import ExitStack
import numpy as np
import concourse.bass as bass
from concourse import mybir

F32 = mybir.dt.float32
F32R = mybir.dt.float32r
BF16 = mybir.dt.bfloat16
I32 = mybir.dt.int32
ALU = mybir.AluOpType
ACT = mybir.ActivationFunctionType
AX = mybir.AxisListType.X

P = 128
S, D, DFF = 512, 1024, 4096
HD = 64
NH = D // HD
NT = S // P
KT = D // P
EPS = 1e-6
NEG = -1e30
ROT = HD // 4
HALF = ROT // 2
THETA = 500000.0
HS = 8
HC = HS * HD
VC = HD + 1
VP = 2 * VC
UP = VP + 2
RAW = 2
WR = 8
LAYOUT = {0: 0, 1: 1, 2: 1}

SETS = [("fox", 0), ("fox", 1), (1, 0), (2, 0), (0, 0), (1, 1), (2, 1), (0, 1)]
SCORE_BANKS = {
    "fox": [[(0, 0, 1), (2, 0, 3)], [(1, 0, 2)], [(3, 0, 4)]],
    0: [[(0, 0, 1), (1, 0, 2)], [(2, 1, 2), (3, 2, 2)]],
    1: [[(r, r, 1) for r in range(NT)]],
    2: [[(r, r, 1) for r in range(NT)]],
}
NB_SET = 12
QK_SET = 8
BANK_FOX = 0
BANK_FOX_OUT = BANK_FOX + 2 * NB_SET
BANK_MLP = [BANK_FOX_OUT + 8, 0]
CHUNKS = DFF // D
BANK_DIL = BANK_MLP[0] + 16 * CHUNKS
BANK_DIL_OUT = BANK_DIL + 6 * NB_SET
BANK_MLP[1] = BANK_DIL_OUT + 8
N_BANKS = BANK_MLP[1] + 16 * CHUNKS


def set_bank0(s):
    return BANK_FOX + NB_SET * s if s < 2 else BANK_DIL + NB_SET * (s - 2)


def ticks_of(s):
    banks = SCORE_BANKS[SETS[s][0]]
    return [(h, i, i == len(banks) - 1) for h in range(HS) for i in range(len(banks))]


TICK0 = [0]
for _s in range(len(SETS)):
    TICK0.append(TICK0[-1] + len(ticks_of(_s)))


def step_plan(proj, attend):
    n = len(ticks_of(attend)) + 3 if attend is not None else 1
    return n


def terms_of_tick(a, n):
    total = NB_SET * 3 * KT
    return range(a * total // n, (a + 1) * total // n)


def banks_of_tick(a, n):
    return [t // (3 * KT) for t in terms_of_tick(a, n) if t % (3 * KT) == 3 * KT - 1]


def head_cols(h):
    return slice((h % 2) * VC, (h % 2) * VC + VC)


def value_cols(h):
    return slice(1 + (h % 2) * HD, 1 + (h % 2) * HD + HD)


def own_values(h):
    return slice(1 - h % 2, 1 - h % 2 + HD)


def own_one(h):
    return (h % 2) * HD


STEPS_FOX = [(0, None), (1, 0), (None, 1)]
STEPS_DIL = [(2, None), (3, 2), (4, 3), (5, 4), (6, 5), (7, 6), (None, 7)]


def trunk(nc, x, positions, fox_norm, fox_w_in, fox_b_f, fox_q_gain, fox_k_gain, fox_w_out,
          dil_norm, dil_w_in, dil_q_gain, dil_k_gain, dil_w_out, mlp_norm, mlp_w1, mlp_w2, out, upto=99):
    ctx = ExitStack()
    with ctx:
        def sb(name, shape, dt=F32, where=ctx):
            return where.enter_context(nc.sbuf_tensor(name, shape, dt))

        def sem(name):
            return ctx.enter_context(nc.semaphore(name))

        act_h = sb("act_h", [P, KT, S], F32R)
        act_l = sb("act_l", [P, KT, S], F32R)
        w_raw = sb("w_raw", [P, RAW, 2, 512])
        w_h = sb("w_h", [P, WR, 2, 512], F32R)
        w_l = sb("w_l", [P, WR, 2, 512], F32R)
        with ExitStack() as once:
            qT = [sb(f"qT{i}", [P, HS // 2, S], F32, once) for i in range(2)]
            kT = [sb(f"kT{i}", [P, HS // 2, S], F32, once) for i in range(2)]
        hid_h = sb("hid_h", [P, KT, S], F32R)
        hid_l = sb("hid_l", [P, KT, S], F32R)
        v_sb = [sb(f"v{i}", [P, NT, HS // 2, VP]) for i in range(2)]
        with ExitStack() as once:
            acc12 = sb("acc12", [P, NT, HS // 2, UP], F32, once)
            o_ring = sb("o_ring", [P, 2, NT, VC], F32, once)
            rt = sb("rt", [P, 2, HS, ROT], F32, once)
        x_sb = sb("x_sb", [P, NT, D])
        with ExitStack() as once:
            gw_raw = sb("gw_raw", [P, KT, P], F32, once)
            gw_h = sb("gw_h", [P, KT, P], F32R, once)
            gw_l = sb("gw_l", [P, KT, P], F32R, once)
        o_sb = sb("o_sb", [P, NT, NH // 2, UP])
        sq = sb("sq", [P, 512])
        qn = sb("qn", [P, 2, 512])
        p_sb = sb("p_sb", [P, 2, 512])
        pT_sb = sb("pT_sb", [P, 2, 512])
        ident = sb("ident", [P, P])
        ident_b = sb("ident_b", [P, P], BF16)
        causal = sb("causal", [P, 512], BF16)
        banded = sb("banded", [P, 256], BF16)
        residue = causal[:, 0:P]
        pick = sb("pick", [P, NH], BF16)
        with ExitStack() as once:
            cos2 = sb("cos2", [P, 2, NT, ROT], F32, once)
            sin2 = sb("sin2", [P, 2, NT, ROT], F32, once)
        c_parts = sb("c_parts", [P, S], BF16)
        diag = sq[:, 0:2 * P].rearrange("p (a b) -> p a b", a=2)
        gain_t = sb("gain_t", [P, 4, KT])
        hg = sb("hg", [P, 8])
        b_f = sb("b_f", [P, 1])
        xss = sb("xss", [P, 16])
        xrs = sb("xrs", [P, 16])
        qss = sb("qss", [P, 2, HS])
        qrs = sb("qrs", [P, 2, HS])
        m_half = sb("m_half", [P, HS])
        negmax = sb("negmax", [P, 6, HS, NT])
        e_arg = sb("e_arg", [P, 4, 2, NT])
        e_fac = sb("e_fac", [P, 4, 2, NT])
        rden = sb("rden", [P, 2, NT])
        rot_g = sb("rot_g", [P, 6, ROT])
        tab_a = sb("tab_a", [P, 6, NT, ROT])
        tab_b = sb("tab_b", [P, 6, NT, ROT])
        pos_i = sb("pos_i", [P, 2, NT], I32)
        pos_f = sb("pos_f", [P, 2 * NT])
        freq = sb("freq", [P, HALF])
        ang = sb("ang", [P, 2 * NT, HALF])
        turns = sb("turns", [P, 2 * NT, HALF])
        sin_t = sb("sin_t", [P, 2 * NT, HALF])
        sinh_t = turns

        ps = [ctx.enter_context(nc.psum_tensor(f"ps{i}", [P, 512], F32)) for i in range(8)]
        ps_proj, ps_q, ps_s, ps_p, ps_o = ps[0:2], ps[2], ps[3:5], ps[5:7], ps[7]
        o_ps = ps_o[:, 0:NT * VC].rearrange("p (t c) -> p t c", c=VC)
        x_dram = nc.dram_tensor("x_kept", (S, D), F32, kind="Internal").ap()
        acc_dram = nc.dram_tensor("acc_kept", (S, HS // 2 * UP), F32, kind="Internal").ap()

        raw_in = [sem(f"raw_in{i}") for i in range(RAW)]
        small_in, hgain_in, gate_in, pos_in = sem("small_in"), sem("hgain_in"), sem("gate_in"), sem("pos_in")
        x_in = [sem(f"x_in{t}") for t in range(NT)]
        wh_done, wl_done = sem("wh_done"), sem("wl_done")
        proj_full = sem("proj_full")
        gwh_done, gwl_done, gate_full, softplus_done = sem("gwh_done"), sem("gwl_done"), sem("gate_full"), sem("softplus_done")
        consts_done, pool_done, tables_done, angle_done, sin_done = (
            sem("consts_done"), sem("pool_done"), sem("tables_done"), sem("angle_done"), sem("sin_done"))
        xss_done, xrs_done, diag_done, prep_full, scaled_done, acth_done, actl_done = (
            sem("xss_done"), sem("xrs_done"), sem("diag_done"), sem("prep_full"), sem("scaled_done"), sem("acth_done"), sem("actl_done"))
        sq_done, qss_done, qrs_done, qn_done, rope_done, qt_full, qt_done, v_done = (
            sem("sq_done"), sem("qss_done"), sem("qrs_done"), sem("qn_done"), sem("rope_done"), sem("qt_full"), sem("qt_done"), sem("v_done"))
        s_full, max_done, exp_done, pt_full, pt_done, pv_done, o_done = (
            sem("s_full"), sem("max_done"), sem("exp_done"), sem("pt_full"), sem("pt_done"), sem("pv_done"), sem("o_done"))
        earg_done, efac_done, merged, normed = sem("earg_done"), sem("efac_done"), sem("merged"), sem("normed")
        acc_out, acc_in, x_out, x_back = sem("acc_out"), sem("acc_in"), sem("x_out"), sem("x_back")
        relu_done, sqr_done, hidh_done, hidl_done, x_added = (
            sem("relu_done"), sem("sqr_done"), sem("hidh_done"), sem("hidl_done"), sem("x_added"))
        dve_own, pool_own, act_own, out_done = sem("dve_own"), sem("pool_own"), sem("act_own"), sem("out_done")

        def f(ap):
            return ap.bitcast(F32)

        def tok(act, k, tile, layout):
            if layout == 0:
                return act[:, k, tile * P:(tile + 1) * P]
            return act[:, k, :].rearrange("p (i r) -> p r i", r=NT)[:, tile, :]

        PREP_OF_NORM = [0, 2, 3, 5]
        X_ADDS = [0, 8, 8 + 8 * CHUNKS, 16 + 8 * CHUNKS]

        def x_ready(eng, norm, t):
            if norm == 0:
                eng.wait_ge(x_in[t], 16)
            else:
                eng.wait_ge(x_added, X_ADDS[norm] - (NT - 1) + t)

        def bank_kind(B):
            for s in range(len(SETS)):
                b = B - set_bank0(s)
                if 0 <= b < NB_SET:
                    return ("qk", QK_SET * s + b) if b < QK_SET else ("v", 4 * s + b - QK_SET)
            if BANK_FOX_OUT <= B < BANK_FOX_OUT + 8:
                return "x", B - BANK_FOX_OUT
            if BANK_DIL_OUT <= B < BANK_DIL_OUT + 8:
                return "x", 8 + 8 * CHUNKS + B - BANK_DIL_OUT
            layer = 0 if B < BANK_DIL else 1
            i, j = divmod(B - BANK_MLP[layer], 16)
            if j < 8:
                return "hid", 8 * CHUNKS * layer + 8 * i + j
            return "x", 8 + (8 * CHUNKS + 8) * layer + 8 * i + j - 8

        def wait_bank_free(pe, B):
            if B >= 2:
                kind, n = bank_kind(B - 2)
                pe.wait_ge({"qk": qn_done, "v": v_done, "hid": sqr_done, "x": x_added}[kind], n + 1)

        block = ctx.enter_context(nc.Block())

        @block.sync
        def _(sp):
            def unit(u, u_more, src):
                if u >= RAW:
                    sp.wait_ge(wl_done, u_more + (u - RAW + 1))
                sp.dma_start(w_raw[:, u % RAW, :, :], src).then_inc(raw_in[u % RAW], 16)

            def group(u, u_more, w, row, col):
                for j in range(4):
                    unit(u + j, u_more, w[bass.ds(row + 2 * j * P, 2 * P), bass.ds(col, 512)]
                         .rearrange("(k p) n -> p k n", p=P))

            def set_groups(s):
                kind, half = SETS[s]
                w = fox_w_in[0] if kind == "fox" else dil_w_in[0]
                base = 0 if kind == "fox" else 3 * D * kind
                for n in range(3):
                    group(set_bank0(s) + 4 * n, 0, w, 0, base + n * D + half * HC)

            def mlp_groups(layer):
                with sp.Fori(0, CHUNKS) as i:
                    b = BANK_MLP[layer]
                    group(b, i * 16, mlp_w1[layer], 0, i * D)
                    group(b + 4, i * 16, mlp_w1[layer], 0, i * D + 512)
                    group(b + 8, i * 16, mlp_w2[layer], i * D, 0)
                    group(b + 12, i * 16, mlp_w2[layer], i * D, 512)

            for t in range(NT):
                sp.dma_start(x_sb[:, t, :], x[0, t * P:(t + 1) * P, :]).then_inc(x_in[t], 16)
            set_groups(0)
            set_groups(1)
            for n in range(2):
                group(BANK_FOX_OUT + 4 * n, 0, fox_w_out[0], 0, 512 * n)
            mlp_groups(0)
            if upto > 1:
                for s in range(2, 8):
                    set_groups(s)
                for n in range(2):
                    group(BANK_DIL_OUT + 4 * n, 0, dil_w_out[0], 0, 512 * n)
                mlp_groups(1)
            total = 8 + 8 * CHUNKS if upto == 1 else 16 + 16 * CHUNKS
            for t in range(NT):
                sp.wait_ge(x_added, total - (NT - 1) + t)
                sp.dma_start(out[0, t * P:(t + 1) * P, :], x_sb[:, t, :]).then_inc(out_done, 16)
            sp.wait_ge(out_done, 16 * NT)

        @block.tensor
        def _(pe):
            mm = nc.tensor.matmul

            def product(ps_out, k, term, lhs, rhs):
                i, j = [(0, 0), (1, 0), (0, 1)][term]
                return mm(ps_out, lhs[i], rhs[j], start=(k == 0 and term == 0), stop=(k == KT - 1 and term == 2))

            def weights_ready(B, k, more=0):
                if k % 2 == 0 and B % 4 == 0:
                    pe.wait_ge(wl_done, more + (B + k // 2 + 1))

            def token_bank(B, k, term, tile, layout=0):
                slot = (B // 4 * 4 + k // 2) % WR
                if term == 0:
                    weights_ready(B, k)
                    if k == 0:
                        wait_bank_free(pe, B)
                return product(ps_proj[B % 2][:, :], k, term, (tok(act_h, k, tile, layout), tok(act_l, k, tile, layout)),
                               (w_h[:, slot, k % 2, :], w_l[:, slot, k % 2, :]))

            def prepare(n, norm):
                for t in range(NT):
                    if norm is not None:
                        pe.wait_ge(diag_done, 4 * norm + t + 1)
                    for half in range(2):
                        pc = 8 * n + 2 * t + half
                        if pc % 8 >= 2:
                            pe.wait_ge(actl_done, pc - 1)
                        for i in range(4):
                            col = ps_p[pc % 2][:, i * P:(i + 1) * P]
                            if norm is not None:
                                c = (4 * half + i) * P
                                last = mm(col, x_sb[:, t, c:c + P], diag[:, t % 2, :], start=True, stop=True)
                            else:
                                last = nc.tensor.transpose(col, o_sb[:, t, 4 * half + i, 1:1 + P], ident[:, :])
                        last.then_inc(prep_full, 1)

            def scores(s, a):
                kind, half = SETS[s]
                h, i, _ = ticks_of(s)[a - TICK0[s]]
                rows = slice(HD * (h % 2), HD * (h % 2) + HD)
                if a >= 2:
                    pe.wait_ge(exp_done, a - 1)
                col = 0
                for q, k0, nk in SCORE_BANKS[kind][i]:
                    n = nk * P
                    dst = ps_s[a % 2][:, col:col + n]
                    mask = (causal[:, 512 - n:512] if kind in ("fox", 1) else
                            banded[:, 256 - n:256] if kind == 0 else residue)
                    mm(dst, ident_b[:, :], mask, start=True, stop=False)
                    if kind == "fox":
                        hh = HS * half + h
                        mm(dst, pick[:, hh:hh + 1].broadcast_to([P, P]), c_parts[:, k0 * P:k0 * P + n], start=False, stop=False)
                    last = mm(dst, qT[s % 2][rows, h // 2, q * P:(q + 1) * P],
                              kT[s % 2][rows, h // 2, k0 * P:k0 * P + n], start=False, stop=True)
                    col += n
                last.then_inc(s_full, 1)

            def width(s, a):
                return sum(nk for _, _, nk in SCORE_BANKS[SETS[s][0]][ticks_of(s)[a - TICK0[s]][1]])

            def turn_probs(s, a):
                pe.wait_ge(exp_done, a + 1)
                if a >= 2:
                    pe.wait_ge(pt_done, a - 1)
                for c in range(width(s, a)):
                    last = nc.tensor.transpose(ps_p[a % 2][:, c * P:(c + 1) * P], p_sb[:, a % 2, c * P:(c + 1) * P], ident[:, :])
                last.then_inc(pt_full, 1)

            def values(s, a):
                h, i, _ = ticks_of(s)[a - TICK0[s]]
                pe.wait_ge(pt_done, a + 1)
                if i == 0 and HS * s + h > 0:
                    pe.wait_ge(o_done, HS * s + h)
                if a == TICK0[s]:
                    pe.wait_ge(v_done, 4 * (s + 1))
                c = 0
                for q, k0, nk in SCORE_BANKS[SETS[s][0]][i]:
                    for k in range(nk):
                        last = mm(o_ps[:, q, 0:VC], pT_sb[:, a % 2, c * P:(c + 1) * P], v_sb[s % 2][:, k0 + k, h // 2, head_cols(h)],
                                  start=(k == 0), stop=(k == nk - 1))
                        c += 1
                last.then_inc(pv_done, 1)

            def turn_qk(s, b):
                n = QK_SET * s + b
                pe.wait_ge(qn_done if s < 2 else rope_done, n + 1 if s < 2 else n - QK_SET * 2 + 1)
                if n >= 1:
                    pe.wait_ge(qt_done, n)
                for i in range(4):
                    last = nc.tensor.transpose(ps_q[:, i * P:(i + 1) * P], qn[:, n % 2, i * P:(i + 1) * P], ident[:, :])
                last.then_inc(qt_full, 1)

            def step(proj, attend):
                n = step_plan(proj, attend)
                for a in range(n):
                    if attend is not None:
                        t0, nt = TICK0[attend], len(ticks_of(attend))
                        if a == 0:
                            pe.wait_ge(qt_done, QK_SET * (attend + 1))
                        if a < nt:
                            scores(attend, t0 + a)
                        if 1 <= a <= nt:
                            turn_probs(attend, t0 + a - 1)
                        if 2 <= a <= nt + 1:
                            values(attend, t0 + a - 2)
                    if proj is None:
                        continue
                    kind = SETS[proj][0]
                    for m in terms_of_tick(a, n):
                        b, k, term = m // (3 * KT), m // 3 % KT, m % 3
                        B = set_bank0(proj) + b
                        if term == 0 and k == 0 and b < 4 and proj in (0, 2):
                            prep = 0 if proj == 0 else 3
                            pe.wait_ge(actl_done, 8 * prep + (2 * (b + 1) if proj == 0 else 8))
                        last = token_bank(B, k, term, b % 4, 0 if kind == "fox" else LAYOUT[kind])
                        if k == KT - 1 and term == 2:
                            last.then_inc(proj_full, 1)
                            if 1 <= b <= QK_SET:
                                turn_qk(proj, b - 1)

            def out_projection(B0, prep):
                for b in range(8):
                    if b < NT:
                        pe.wait_ge(actl_done, 8 * prep + 2 * (b + 1))
                    for k in range(KT):
                        for term in range(3):
                            last = token_bank(B0 + b, k, term, b % 4)
                    last.then_inc(proj_full, 1)

            def mlp(layer):
                B0 = BANK_MLP[layer]
                pe.wait_ge(actl_done, 8 * (2 if layer == 0 else 5) + 8)
                with pe.Fori(0, CHUNKS) as i:
                    for b in range(16):
                        B = B0 + b
                        if b in (0, 1):
                            pe.wait_ge(x_added, i * 8 + X_ADDS[1 if layer == 0 else 3] - 1 + b)
                        elif b < 10:
                            pe.wait_ge(sqr_done, i * 8 + (8 * CHUNKS * layer + b - 1))
                        else:
                            pe.wait_ge(x_added, i * 8 + (X_ADDS[1 if layer == 0 else 3] + b - 9))
                        for k in range(KT):
                            slot = (B // 4 * 4 + k // 2) % WR
                            weights_ready(B, k, i * 16)
                            w = (w_h[:, slot, k % 2, :], w_l[:, slot, k % 2, :])
                            if b < 8:
                                c = slice((b % 4) * P, (b % 4 + 1) * P)
                                lhs, rhs = (w[0][:, c], w[1][:, c]), (act_h[:, k, :], act_l[:, k, :])
                            else:
                                if b == 8:
                                    pe.wait_ge(hidl_done, i * 8 + (8 * CHUNKS * layer + k + 1))
                                c = slice((b % 4) * P, (b % 4 + 1) * P)
                                lhs, rhs = (hid_h[:, k, c], hid_l[:, k, c]), w
                            for term in range(3):
                                last = product(ps_proj[B % 2][:, :], k, term, lhs, rhs)
                        last.then_inc(proj_full, 1)

            pe.wait_ge(consts_done, 1)
            prepare(0, 0)
            pe.wait_ge(gwl_done, 1)
            pe.wait_ge(actl_done, 8)
            for k in range(KT):
                for term in range(3):
                    last = product(ps_o[:, :], k, term, (gw_h[:, k, :], gw_l[:, k, :]), (act_h[:, k, :], act_l[:, k, :]))
            last.then_inc(gate_full, 1)
            for n, (proj, attend) in enumerate(STEPS_FOX):
                if n == 1:
                    pe.wait_ge(softplus_done, 3)
                step(proj, attend)
            pe.wait_ge(o_done, 2 * HS)
            prepare(1, None)
            out_projection(BANK_FOX_OUT, 1)
            prepare(2, 1)
            mlp(0)
            if upto > 1:
                prepare(3, 2)
                for proj, attend in STEPS_DIL:
                    step(proj, attend)
                pe.wait_ge(normed, 2 * HS)
                prepare(4, None)
                out_projection(BANK_DIL_OUT, 4)
                prepare(5, 3)
                mlp(1)

        @block.scalar
        def _(act):
            fn = nc.scalar.activation
            own = [0]

            def link(ins):
                own[0] += 1
                ins.then_inc(act_own, 1)
                act.wait_ge(act_own, own[0])

            def split_high(u, more=0, raws=0):
                act.wait_ge(raw_in[u % RAW], raws + 16 * (u // RAW + 1))
                if u // 4 >= 2:
                    act.wait_ge(proj_full, more + 4 * (u // 4 - 1))
                nc.scalar.copy(w_h[:, u % WR, :, :], w_raw[:, u % RAW, :, :]).then_inc(wh_done, 1)

            def norm_sums(norm):
                for t in range(NT):
                    n = 4 * norm + t
                    x_ready(act, norm, t)
                    if n > 0:
                        act.wait_ge(xss_done, n)
                    fn(pT_sb[:, :, :].rearrange("p a b -> p (a b)"), x_sb[:, t, :], ACT.Square,
                       accum_out=xss[:, n:n + 1]).then_inc(xss_done, 1)

            def prepare(n, norm):
                for pc in range(8 * n, 8 * n + 8):
                    t, half = pc % 8 // 2, pc % 2
                    if norm is not None:
                        act.wait_ge(scaled_done, 8 * norm + pc % 8 + 1)
                        src = qn[:, pc % 2, :]
                    else:
                        act.wait_ge(prep_full, pc + 1)
                        src = ps_p[pc % 2][:, :]
                    nc.scalar.copy(act_h[:, 4 * half:4 * half + 4, t * P:(t + 1) * P],
                                   src.rearrange("p (k t) -> p k t", k=4)).then_inc(acth_done, 1)

            def qk_evacuate(s, b):
                kind, _ = SETS[s]
                n = QK_SET * s + b
                if b == 0 and s >= 2:
                    act.wait_ge(pv_done, TICK0[s - 1])
                act.wait_ge(qt_full, n + 1)
                g = (0 if kind == "fox" else 2 + 2 * kind) + b // 4
                dst = (qT if b < 4 else kT)[s % 2][:, :, (b % 4) * P:(b % 4 + 1) * P]
                fn(dst, ps_q[:, :].rearrange("p (i t) -> p i t", i=4), ACT.Copy, scale=hg[:, g:g + 1]).then_inc(qt_done, 1)

            def bank_event(s, b):
                B = set_bank0(s) + b
                split_high(B + 4)
                act.wait_ge(proj_full, B + 1)
                src = ps_proj[B % 2][:, :]
                if b < QK_SET:
                    n = QK_SET * s + b
                    if n >= 1:
                        act.wait_ge(qss_done, n)
                    fn(sq[:, :], src, ACT.Square).then_inc(sq_done, 1)
                else:
                    if b == QK_SET and s >= 2:
                        act.wait_ge(pv_done, TICK0[s - 1])
                    nc.scalar.copy(v_sb[s % 2][:, b - QK_SET, :, 1:1 + P],
                                   src.rearrange("p (h d) -> p h d", d=P)).then_inc(v_done, 1)
                if 1 <= b <= QK_SET:
                    qk_evacuate(s, b - 1)

            merges = [0]

            def probs(s, a):
                kind, half = SETS[s]
                h, i, last_bank = ticks_of(s)[a - TICK0[s]]
                act.wait_ge(max_done, a + 1)
                if a >= 2:
                    act.wait_ge(pt_full, a - 1)
                col = 0
                for q, _, nk in SCORE_BANKS[kind][i]:
                    c = slice(col, col + nk * P)
                    last = fn(p_sb[:, a % 2, c], ps_s[a % 2][:, c], ACT.Exp, bias=negmax[:, s % 6, h, q:q + 1])
                    col += nk * P
                last.then_inc(exp_done, 1)
                if kind in (2, 0) and last_bank:
                    m = merges[0]
                    act.wait_ge(earg_done, m + 1)
                    if m >= 4:
                        act.wait_ge(merged, m - 3)
                    fn(e_fac[:, m % 4, :, :], e_arg[:, m % 4, :, :], ACT.Exp).then_inc(efac_done, 1)
                    merges[0] += 1

            def step(proj, attend):
                n = step_plan(proj, attend)
                for a in range(n):
                    if attend is not None and a < len(ticks_of(attend)):
                        probs(attend, TICK0[attend] + a)
                    if proj is not None:
                        for b in banks_of_tick(a, n):
                            bank_event(proj, b)

            def mlp(layer):
                B0, h0 = BANK_MLP[layer], 8 * CHUNKS * layer

                def hidden_high(i, j):
                    act.wait_ge(sqr_done, i * 8 + (h0 + j + 1))
                    nc.scalar.copy(hid_h[:, j, :], p_sb[:, j % 2, :]).then_inc(hidh_done, 1)

                def chunk(i, final):
                    for b in range(16):
                        B = B0 + b
                        if not (final and b >= 12):
                            split_high(B + 4, i * 16, i * (16 * 16 // RAW))
                        if b < 8:
                            act.wait_ge(proj_full, i * 16 + (B + 1))
                            fn(qn[:, b % 2, :], ps_proj[B % 2][:, :], ACT.Relu).then_inc(relu_done, 1)
                        if 1 <= b <= 8:
                            hidden_high(i, b - 1)

                if layer == 0 and upto > 1:
                    with act.Fori(0, CHUNKS) as i:
                        chunk(i, False)
                else:
                    with act.Fori(0, CHUNKS - 1) as i:
                        chunk(i, False)
                    chunk(CHUNKS - 1, True)

            act.dma_start(gw_raw[:, :, 0:NH], fox_w_in[0][:, 3 * D:3 * D + NH].rearrange("(k p) n -> p k n", p=P)).then_inc(gate_in, 16)
            act.dma_start(gw_raw[:, :, NH:P], fox_w_in[0][:, 0:P - NH].rearrange("(k p) n -> p k n", p=P)).then_inc(gate_in, 16)
            norms = [fox_norm[0], mlp_norm[0], dil_norm[0], mlp_norm[1]]
            for n in range(4):
                act.dma_start(gain_t[:, n, :], norms[n].rearrange("(k p) -> p k", p=P), allow_slow_non_contiguous=True).then_inc(small_in, 16)
            act.dma_start(b_f[0:NH, :], fox_b_f[0].rearrange("(h a) -> h a", a=1)).then_inc(small_in, 16)
            norm_sums(0)
            act.wait_ge(gate_in, 32)
            nc.scalar.copy(gw_h[:, :, :], gw_raw[:, :, :]).then_inc(gwh_done, 1)
            prepare(0, 0)
            for u in range(4):
                split_high(u)
            act.wait_ge(hgain_in, 1)
            step(*STEPS_FOX[0])
            act.wait_ge(softplus_done, 1)
            link(fn(p_sb[0:NH, 0, :], pT_sb[0:NH, 0, :], ACT.Abs))
            link(fn(p_sb[0:NH, 1, :], p_sb[0:NH, 0, :], ACT.Exp, scale=-1.0))
            fn(p_sb[0:NH, 0, :], p_sb[0:NH, 1, :], ACT.Ln, bias=1.0).then_inc(softplus_done, 1)
            act.wait_ge(softplus_done, 3)
            step(*STEPS_FOX[1])
            step(*STEPS_FOX[2])
            if upto > 1:
                act.wait_ge(angle_done, 1)
                fn(sin_t[:, :, :], ang[:, :, :], ACT.Sin)
                fn(sinh_t[:, :, :], ang[:, :, :], ACT.Sin, scale=0.5).then_inc(sin_done, 1)
            prepare(1, None)
            for b in range(8):
                split_high(BANK_FOX_OUT + b + 4)
            norm_sums(1)
            prepare(2, 1)
            mlp(0)
            if upto > 1:
                norm_sums(2)
                act.dma_start(x_dram.rearrange("(t p) d -> p t d", p=P), x_sb[:, :, :]).then_inc(x_out, 16)
                prepare(3, 2)
                for proj, attend in STEPS_DIL:
                    step(proj, attend)
                act.wait_ge(merged, 4 * HS)
                act.wait_ge(x_out, 16)
                act.dma_start(x_sb[:, :, :], x_dram.rearrange("(t p) d -> p t d", p=P)).then_inc(x_back, 16)
                prepare(4, None)
                for b in range(8):
                    split_high(BANK_DIL_OUT + b + 4)
                norm_sums(3)
                prepare(5, 3)
                mlp(1)

        @block.vector
        def _(dve):
            v = nc.vector
            own = [0]

            def link(ins):
                own[0] += 1
                ins.then_inc(dve_own, 1)
                dve.wait_ge(dve_own, own[0])

            def split_low(u, more=0):
                dve.wait_ge(wh_done, more + (u + 1))
                v.tensor_tensor(w_l[:, u % WR, :, :], w_raw[:, u % RAW, :, :], f(w_h[:, u % WR, :, :]), ALU.subtract).then_inc(wl_done, 1)

            def prepare(n, norm):
                def low(pc):
                    t, half = pc % 8 // 2, pc % 2
                    dst = (slice(None), slice(4 * half, 4 * half + 4), slice(t * P, (t + 1) * P))
                    src = qn[:, pc % 2, :] if norm is not None else ps_p[pc % 2][:, :]
                    dve.wait_ge(acth_done, pc + 1)
                    v.tensor_tensor(act_l[dst], src.rearrange("p (k t) -> p k t", k=4), f(act_h[dst]), ALU.subtract).then_inc(actl_done, 1)

                for j in range(9):
                    pc = 8 * n + j
                    t, half = j // 2, j % 2
                    if norm is not None and j < 8:
                        if half == 0:
                            m = 4 * norm + t
                            dve.wait_ge(xrs_done, m + 1)
                            if t >= 2:
                                dve.wait_ge(prep_full, 8 * n + 2 * (t - 1))
                            v.tensor_scalar(diag[:, t % 2, :], ident[:, :], xrs[:, m:m + 1], None, ALU.mult).then_inc(diag_done, 1)
                    if norm is not None and j < 8:
                        dve.wait_ge(prep_full, pc + 1)
                        if j >= 2:
                            dve.wait_ge(actl_done, pc - 1)
                        g = gain_t[:, norm, 4 * half:4 * half + 4].unsqueeze(2).broadcast_to([P, 4, P])
                        v.tensor_tensor(qn[:, pc % 2, :].rearrange("p (k t) -> p k t", k=4),
                                        ps_p[pc % 2][:, :].rearrange("p (k t) -> p k t", k=4), g, ALU.mult).then_inc(scaled_done, 1)
                    if j >= 1:
                        low(pc - 1)

            def bank_event(s, b):
                B = set_bank0(s) + b
                if b < QK_SET:
                    n = QK_SET * s + b
                    dve.wait_ge(sq_done, n + 1)
                    if n >= 2:
                        dve.wait_ge(qrs_done, n - 1)
                    v.tensor_reduce(qss[:, n % 2, :], sq[:, :].rearrange("p (h d) -> p h d", d=HD), AX, ALU.add).then_inc(qss_done, 1)
                split_low(B + 4)
                if b < QK_SET:
                    dve.wait_ge(qrs_done, n + 1)
                    if n >= 2:
                        dve.wait_ge(qt_full, n - 1)
                    v.tensor_tensor(qn[:, n % 2, :].rearrange("p (h d) -> p h d", d=HD),
                                    ps_proj[B % 2][:, :].rearrange("p (h d) -> p h d", d=HD),
                                    qrs[:, n % 2, :].unsqueeze(2).broadcast_to([P, HS, HD]), ALU.mult).then_inc(qn_done, 1)

            merges = [0]

            def maxima(s, a):
                kind, half = SETS[s]
                h, i, last_bank = ticks_of(s)[a - TICK0[s]]
                dve.wait_ge(s_full, a + 1)
                segs = SCORE_BANKS[kind][i]
                if len({nk for _, _, nk in segs}) == 1:
                    q0, nk = segs[0][0], segs[0][2]
                    last = v.tensor_reduce(negmax[:, s % 6, h, q0:q0 + len(segs)],
                                           ps_s[a % 2][:, 0:len(segs) * nk * P].rearrange("p (q k) -> p q k", k=nk * P),
                                           AX, ALU.max, negate=True)
                else:
                    col = 0
                    for q, _, nk in segs:
                        last = v.tensor_reduce(negmax[:, s % 6, h, q:q + 1], ps_s[a % 2][:, col:col + nk * P], AX, ALU.max, negate=True)
                        col += nk * P
                last.then_inc(max_done, 1)
                if kind in (2, 0) and last_bank:
                    m = merges[0]
                    dve.wait_ge(max_done, a + 1)
                    mine = negmax[:, s % 6, h, :]
                    if kind == 2:
                        other, both = negmax[:, (s - 1) % 6, h, :], acc12[:, :, h // 2, VP + h % 2]
                    else:
                        if h == 0:
                            dve.wait_ge(acc_in, 16 * (half + 1))
                        other = both = o_sb[:, :, (HS * half + h) // 2, VP + h % 2]
                    if kind == 2:
                        link(v.tensor_tensor(both, mine, other, ALU.min))
                        v.tensor_tensor(e_arg[:, m % 4, 0, :], both, other, ALU.subtract)
                        v.tensor_tensor(e_arg[:, m % 4, 1, :], both, mine, ALU.subtract).then_inc(earg_done, 1)
                    else:
                        link(v.tensor_tensor(rden[:, 0, :], mine, other, ALU.min))
                        v.tensor_tensor(e_arg[:, m % 4, 0, :], rden[:, 0, :], other, ALU.subtract)
                        v.tensor_tensor(e_arg[:, m % 4, 1, :], rden[:, 0, :], mine, ALU.subtract).then_inc(earg_done, 1)
                    merges[0] += 1

            def probs_back(s, a):
                w = P * sum(nk for _, _, nk in SCORE_BANKS[SETS[s][0]][ticks_of(s)[a - TICK0[s]][1]])
                dve.wait_ge(pt_full, a + 1)
                if a >= 2:
                    dve.wait_ge(pv_done, a - 1)
                v.tensor_copy(pT_sb[:, a % 2, 0:w], ps_p[a % 2][:, 0:w]).then_inc(pt_done, 1)

            evacuated = [0]

            def output(s, a):
                kind, half = SETS[s]
                h, _, last_bank = ticks_of(s)[a - TICK0[s]]
                if not last_bank:
                    return
                dve.wait_ge(pv_done, a + 1)
                if kind == "fox":
                    link(v.reciprocal(rden[:, 0, :], o_ps[:, :, own_one(h)]))
                    v.tensor_tensor(o_sb[:, :, (HS * half + h) // 2, value_cols(h)], o_ps[:, :, own_values(h)],
                                    rden[:, 0, :].unsqueeze(2).broadcast_to([P, NT, HD]), ALU.mult).then_inc(o_done, 1)
                elif kind == 1:
                    if h == 0:
                        if half == 0:
                            dve.wait_ge(x_out, 16)
                        else:
                            dve.wait_ge(acc_out, 16)
                    v.tensor_copy(acc12[:, :, h // 2, head_cols(h)], o_ps[:, :, 0:VC]).then_inc(o_done, 1)
                else:
                    m = evacuated[0]
                    if m >= 2:
                        dve.wait_ge(merged, m - 1)
                    v.tensor_copy(o_ring[:, m % 2, :, 0:VC], o_ps[:, :, 0:VC]).then_inc(o_done, 1)
                    evacuated[0] += 1

            def normalise(s, h):
                half = SETS[s][1]
                m = 2 * HS * half + HS + h
                dve.wait_ge(merged, m + 1)
                o = o_sb[:, :, (HS * half + h) // 2, head_cols(h)]
                link(v.reciprocal(rden[:, 1, :], o[:, :, own_one(h)]))
                v.tensor_tensor(o[:, :, own_values(h)], o[:, :, own_values(h)], rden[:, 1, :].unsqueeze(2).broadcast_to([P, NT, HD]), ALU.mult).then_inc(normed, 1)

            def step(proj, attend):
                n = step_plan(proj, attend)
                for a in range(n):
                    if attend is not None:
                        t0, nt, tl = TICK0[attend], len(ticks_of(attend)), ticks_of(attend)
                        if a < nt:
                            maxima(attend, t0 + a)
                        if 1 <= a <= nt:
                            probs_back(attend, t0 + a - 1)
                        if 3 <= a and SETS[attend][0] == 0 and tl[a - 3][2]:
                            normalise(attend, tl[a - 3][0])
                        if 2 <= a <= nt + 1:
                            output(attend, t0 + a - 2)
                    if proj is not None:
                        for b in banks_of_tick(a, n):
                            bank_event(proj, b)

            def x_add(B, t, half, count, more=0):
                dve.wait_ge(proj_full, more + (B + 1))
                if count is not None:
                    dve.wait_ge(x_added, count)
                dst = x_sb[:, t, half * 512:(half + 1) * 512]
                v.tensor_tensor(dst, ps_proj[B % 2][:, :], dst, ALU.add).then_inc(x_added, 1)

            def out_projection(B0):
                for b in range(8):
                    split_low(B0 + b + 4)
                    x_add(B0 + b, b % 4, b // 4, None)

            def mlp(layer):
                B0, h0 = BANK_MLP[layer], 8 * CHUNKS * layer

                def hidden_low(i, j):
                    dve.wait_ge(hidh_done, i * 8 + (h0 + j + 1))
                    v.tensor_tensor(hid_l[:, j, :], p_sb[:, j % 2, :], f(hid_h[:, j, :]), ALU.subtract).then_inc(hidl_done, 1)

                def chunk(i, final):
                    for b in range(16):
                        B = B0 + b
                        if b < 8:
                            dve.wait_ge(relu_done, i * 8 + (h0 + b + 1))
                            if b >= 2:
                                dve.wait_ge(hidl_done, i * 8 + (h0 + b - 1))
                            v.scalar_tensor_tensor(p_sb[:, b % 2, :], ps_proj[B % 2][:, :], 0.0, qn[:, b % 2, :],
                                                   ALU.max, ALU.mult).then_inc(sqr_done, 1)
                        if not (final and b >= 12):
                            split_low(B + 4, i * 16)
                        if 1 <= b <= 8:
                            hidden_low(i, b - 1)
                        if b >= 8:
                            x_add(B, b % 4, (b - 8) // 4, i * 8 + (X_ADDS[1 if layer == 0 else 3] + b - 8), i * 16)

                if layer == 0 and upto > 1:
                    with dve.Fori(0, CHUNKS) as i:
                        chunk(i, False)
                else:
                    with dve.Fori(0, CHUNKS - 1) as i:
                        chunk(i, False)
                    chunk(CHUNKS - 1, True)

            dve.wait_ge(consts_done, 1)
            dve.wait_ge(small_in, 16 * 5)
            prepare(0, 0)
            dve.wait_ge(gwh_done, 1)
            v.tensor_tensor(gw_l[:, :, :], gw_raw[:, :, :], f(gw_h[:, :, :]), ALU.subtract).then_inc(gwl_done, 1)
            for u in range(4):
                split_low(u)
            step(*STEPS_FOX[0])
            z0, lf, c1, rem = pT_sb[0:NH, 0, :], pT_sb[0:NH, 1, :], p_sb[0:NH, 1, 0:S // 2].bitcast(BF16), sq[0:NH, :]
            dve.wait_ge(gate_full, 1)
            v.tensor_scalar(z0, ps_o[0:NH, :], b_f[0:NH, :], None, ALU.add).then_inc(softplus_done, 1)
            dve.wait_ge(softplus_done, 2)
            link(v.tensor_scalar(z0, z0, 0.0, None, ALU.min))
            link(v.tensor_tensor(lf, z0, p_sb[0:NH, 0, :], ALU.subtract))
            link(v.memset(z0, 1.0))
            link(v.tensor_tensor_scan(rem, z0, lf, 0.0, ALU.mult, ALU.subtract))
            for part in range(3):
                link(v.tensor_copy(c1, rem))
                last = v.tensor_copy(c_parts[32 * part:32 * part + NH, :], c1)
                if part < 2:
                    link(v.tensor_tensor(rem, rem, c1, ALU.subtract))
            last.then_inc(softplus_done, 1)
            step(*STEPS_FOX[1])
            step(*STEPS_FOX[2])
            prepare(1, None)
            out_projection(BANK_FOX_OUT)
            prepare(2, 1)
            mlp(0)
            if upto > 1:
                prepare(3, 2)
                for proj, attend in STEPS_DIL:
                    step(proj, attend)
                prepare(4, None)
                dve.wait_ge(x_back, 16)
                out_projection(BANK_DIL_OUT)
                prepare(5, 3)
                mlp(1)

        @block.gpsimd
        def _(pool):
            g = nc.gpsimd
            own = [0]

            def link(ins):
                own[0] += 1
                ins.then_inc(pool_own, 1)
                pool.wait_ge(pool_own, own[0])

            def select(ap, pattern, base, cm, op, fill):
                link(g.affine_select(out=ap, in_=ap, compare_op=op, fill=fill, base=base, pattern=pattern, channel_multiplier=cm))

            def norm_scale(norm):
                for t in range(NT):
                    n = 4 * norm + t
                    pool.wait_ge(xss_done, n + 1)
                    link(g.tensor_scalar(xss[:, n:n + 1], xss[:, n:n + 1], 1.0 / D, EPS, ALU.mult, ALU.add))
                    g.tensor_tensor(xrs[:, n:n + 1], xss[:, n:n + 1], m_half[:, 0:1], ALU.pow).then_inc(xrs_done, 1)

            def bank_event(s, b):
                if b >= QK_SET:
                    return
                kind, _ = SETS[s]
                n = QK_SET * s + b
                pool.wait_ge(qss_done, n + 1)
                link(g.tensor_scalar(qss[:, n % 2, :], qss[:, n % 2, :], HD * EPS, None, ALU.add))
                g.tensor_tensor(qrs[:, n % 2, :], qss[:, n % 2, :], m_half[:, :], ALU.pow).then_inc(qrs_done, 1)
                if kind == "fox":
                    return
                pool.wait_ge(qn_done, n + 1)
                tab = 2 * kind + b // 4
                rot = qn[:, n % 2, :].rearrange("p (h d) -> p h d", d=HD)[:, :, 0:ROT]
                ta = tab_a[:, tab, b % 4, :].unsqueeze(1).broadcast_to([P, HS, ROT])
                tb = tab_b[:, tab, b % 4, :].unsqueeze(1).broadcast_to([P, HS, ROT])
                g.tensor_tensor(rt[:, 0, :, :], rot, ta, ALU.mult)
                g.tensor_tensor(rt[:, 1, :, 0:HALF], rot[:, :, HALF:ROT], tb[:, :, 0:HALF], ALU.mult)
                link(g.tensor_tensor(rt[:, 1, :, HALF:ROT], rot[:, :, 0:HALF], tb[:, :, HALF:ROT], ALU.mult))
                g.tensor_tensor(rot, rt[:, 0, :, :], rt[:, 1, :, :], ALU.add).then_inc(rope_done, 1)
                pool.wait_ge(rope_done, n - 2 * QK_SET + 1)

            merges = [0]

            def merge(s, a):
                kind, half = SETS[s]
                h, _, last_bank = ticks_of(s)[a - TICK0[s]]
                if kind not in (2, 0) or not last_bank:
                    return
                m = merges[0]
                acc = acc12[:, :, h // 2, head_cols(h)] if kind == 2 else o_sb[:, :, (HS * half + h) // 2, head_cols(h)]
                new = o_ring[:, m % 2, :, 0:VC]
                pool.wait_ge(efac_done, m + 1)
                pool.wait_ge(o_done, HS * s + h + 1)
                g.tensor_tensor(acc, acc, e_fac[:, m % 4, 0, :].unsqueeze(2).broadcast_to([P, NT, VC]), ALU.mult)
                link(g.tensor_tensor(new, new, e_fac[:, m % 4, 1, :].unsqueeze(2).broadcast_to([P, NT, VC]), ALU.mult))
                g.tensor_tensor(acc, acc, new, ALU.add).then_inc(merged, 1)
                merges[0] += 1

            def reorder(half):
                pool.wait_ge(merged, merges[0])
                if half:
                    pool.wait_ge(acc_in, 16)
                pool.dma_start(acc_dram.rearrange("(p r) c -> p r c", r=NT), acc12[:, :, :, :].rearrange("p r h c -> p r (h c)")).then_inc(acc_out, 16)
                pool.wait_ge(acc_out, 16 * (half + 1))
                pool.dma_start(o_sb[:, :, HS // 2 * half:HS // 2 * (half + 1), :].rearrange("p t h c -> p t (h c)"),
                               acc_dram.rearrange("(t p) c -> p t c", p=P)).then_inc(acc_in, 16)

            def step(proj, attend):
                n = step_plan(proj, attend)
                for a in range(n):
                    if attend is not None and 2 <= a <= len(ticks_of(attend)) + 1:
                        merge(attend, TICK0[attend] + a - 2)
                    if proj is not None:
                        for b in banks_of_tick(a, n):
                            bank_event(proj, b)
                if attend is not None and SETS[attend][0] == 2:
                    reorder(SETS[attend][1])

            link(g.memset(ident[:, :], 0.0))
            select(ident[:, :], [[-1, P]], 0, 1, ALU.not_equal, 1.0)
            link(g.memset(m_half[:, :], -0.5))
            link(g.tensor_copy(ident_b[:, :], ident[:, :]))
            g.memset(hg[:, :], 1.0).then_inc(consts_done, 1)
            norm_scale(0)
            pool.wait_ge(consts_done, 1)
            for j, (gain, c) in enumerate([(fox_q_gain[0], 0), (fox_k_gain[0], 1)]
                                          + [(dil_q_gain[0, i], 2 + 2 * i) for i in range(3)]
                                          + [(dil_k_gain[0, i], 3 + 2 * i) for i in range(3)]):
                lo = 0 if c < 2 else ROT
                for r in (0, HD):
                    pool.dma_start(hg[r + lo:r + HD, c:c + 1], gain[lo:HD].rearrange("(d a) -> d a", a=1)).then_inc(pos_in, 16)
            for i in range(3):
                for n, gain in enumerate((dil_q_gain, dil_k_gain)):
                    pool.dma_start(rot_g[:, 2 * i + n, :], gain[0, i:i + 1, 0:ROT].partition_broadcast(P)).then_inc(pos_in, 16)
            pool.dma_start(pos_i[:, 1, :], positions[0].rearrange("(p r) -> p r", r=NT)).then_inc(pos_in, 16)
            pool.dma_start(pos_i[:, 0, :], positions[0].rearrange("(t p) -> p t", p=P), allow_slow_non_contiguous=True).then_inc(pos_in, 16)
            pool.wait_ge(pos_in, 16 * 24)
            kg = hg[:, :].rearrange("p (a b) -> p a b", b=2)[:, :, 1]
            g.tensor_scalar(kg, kg, float(HD) ** 0.5, None, ALU.mult).then_inc(hgain_in, 1)
            link(g.memset(causal[:, :], 0.0))
            select(causal[:, 384:512], [[-1, P]], 0, 1, ALU.is_ge, NEG)
            link(g.memset(banded[:, :], 0.0))
            select(banded[:, 0:P], [[1, P]], 0, -1, ALU.is_ge, NEG)
            select(banded[:, P:2 * P], [[-1, P]], 0, 1, ALU.is_ge, NEG)
            link(g.memset(pick[:, :], 0.0))
            link(g.memset(c_parts[:, :], 0.0))
            for part in range(3):
                select(pick[32 * part:32 * part + NH, :], [[-1, NH]], 0, 1, ALU.not_equal, 1.0)
            for i in range(2):
                link(g.memset(v_sb[i][:, :, :, 0:VP:VP - 1], 1.0))
            step(*STEPS_FOX[0])
            if upto > 1:
                inv = np.float32(THETA) ** (-np.arange(HALF, dtype=np.float32) * np.float32(2.0) / np.float32(ROT))
                for j in range(HALF):
                    g.memset(freq[:, j:j + 1], float(inv[j]))
                link(g.tensor_copy(pos_f[:, :], pos_i[:, :, :].rearrange("p a b -> p (a b)")))
                link(g.tensor_tensor(ang[:, :, :], pos_f[:, :].unsqueeze(2).broadcast_to([P, 2 * NT, HALF]),
                                     freq[:, :].unsqueeze(1).broadcast_to([P, 2 * NT, HALF]), ALU.mult))
                magic = float(1.5 * 2 ** 23)
                link(g.tensor_scalar(turns[:, :, :], ang[:, :, :], 1.0 / (2 * np.pi), magic, ALU.mult, ALU.add))
                link(g.tensor_scalar(turns[:, :, :], turns[:, :, :], magic, None, ALU.subtract))
                two_pi = 2 * np.pi
                c1 = 6.28125
                c2 = float(np.float32(round((two_pi - c1) * 2 ** 19) / 2 ** 19))
                c3 = float(np.float32(two_pi - c1 - c2))
                for c in (c1, c2, c3):
                    link(g.tensor_scalar(sin_t[:, :, :], turns[:, :, :], c, None, ALU.mult))
                    link(g.tensor_tensor(ang[:, :, :], ang[:, :, :], sin_t[:, :, :], ALU.subtract))
                pi_down = 3.1415925
                g.tensor_scalar(ang[:, :, :], ang[:, :, :], pi_down, -pi_down, ALU.min, ALU.max).then_inc(angle_done, 1)
            step(*STEPS_FOX[1])
            step(*STEPS_FOX[2])
            norm_scale(1)
            if upto > 1:
                pool.wait_ge(sin_done, 1)
                link(g.tensor_tensor(sinh_t[:, :, :], sinh_t[:, :, :], sinh_t[:, :, :], ALU.mult))
                st = sin_t[:, :, :].rearrange("p (a t) j -> p a t j", a=2)
                ch = sinh_t[:, :, :].rearrange("p (a t) j -> p a t j", a=2)
                for lay in range(2):
                    for hlf in range(2):
                        c = slice(hlf * HALF, (hlf + 1) * HALF)
                        link(g.tensor_scalar(cos2[:, lay, :, c], ch[:, lay, :, :], -2.0, 1.0, ALU.mult, ALU.add))
                        link(g.tensor_scalar(sin2[:, lay, :, c], st[:, lay, :, :], 2.0 * hlf - 1.0, None, ALU.mult))
                for tab in range(6):
                    lay = LAYOUT[tab // 2]
                    gn = rot_g[:, tab, :]
                    link(g.tensor_tensor(tab_a[:, tab, :, :], cos2[:, lay, :, :], gn.unsqueeze(1).broadcast_to([P, NT, ROT]), ALU.mult))
                    for hlf in range(2):
                        c = slice(hlf * HALF, (hlf + 1) * HALF)
                        o = slice((1 - hlf) * HALF, (2 - hlf) * HALF)
                        link(g.tensor_tensor(tab_b[:, tab, :, c], sin2[:, lay, :, c], gn[:, o].unsqueeze(1).broadcast_to([P, NT, HALF]), ALU.mult))
                pool.wait_ge(pv_done, TICK0[2])
                link(g.memset(residue, NEG))
                for d in range(0, P, NT):
                    select(residue, [[-1, P]], -d, 1, ALU.not_equal, 0.0)
                pool.nop().then_inc(pool_done, 1)
                norm_scale(2)
                pool.wait_ge(x_out, 16)
                for proj, attend in STEPS_DIL:
                    step(proj, attend)
                norm_scale(3)


_INS = ["x", "positions", "fox_norm", "fox_w_in", "fox_b_f", "fox_q_gain", "fox_k_gain", "fox_w_out",
        "dil_norm", "dil_w_in", "dil_q_gain", "dil_k_gain", "dil_w_out", "mlp_norm", "mlp_w1", "mlp_w2"]


def kernel(**inputs):
    from concourse import bacc
    from concourse.bass_utils import run_bass_kernel_spmd

    nc = bacc.Bacc("TRN2", target_bir_lowering=False, num_devices=1)
    arrays, args = {}, []
    for name in _INS:
        a = np.ascontiguousarray(inputs[name])
        arrays[f"in_{name}"] = a
        args.append(nc.dram_tensor(f"in_{name}", a.shape, mybir.dt.from_np(a.dtype), kind="ExternalInput").ap())
    args.append(nc.dram_tensor("out_0", (1, S, D), F32, kind="ExternalOutput").ap())
    trunk(nc, *args)
    r = run_bass_kernel_spmd(nc, [arrays], core_ids=[0])
    return r.results[0]["out_0"]
```

```python
from contextlib import ExitStack
import numpy as np
import concourse.bass as bass
from concourse import mybir

F32 = mybir.dt.float32
F32R = mybir.dt.float32r
BF16 = mybir.dt.bfloat16
I32 = mybir.dt.int32
ALU = mybir.AluOpType
ACT = mybir.ActivationFunctionType
AX = mybir.AxisListType.X

P = 128
S, D, DFF = 512, 1024, 4096
HD = 64
NH = D // HD
NT = S // P
KT = D // P
EPS = 1e-6
NEG = -1e30
ROT = HD // 4
HALF = ROT // 2
THETA = 500000.0
HS = 8
HC = HS * HD
VC = HD + 1
VP = 2 * VC
UP = VP + 2
RAW = 2
WR = 8
LAYOUT = {0: 0, 1: 1, 2: 1}

SETS = [("fox", 0), ("fox", 1), (1, 0), (2, 0), (0, 0), (1, 1), (2, 1), (0, 1)]
SCORE_BANKS = {
    "fox": [[(0, 0, 1), (2, 0, 3)], [(1, 0, 2)], [(3, 0, 4)]],
    0: [[(0, 0, 1), (1, 0, 2)], [(2, 1, 2), (3, 2, 2)]],
    1: [[(r, r, 1) for r in range(NT)]],
    2: [[(r, r, 1) for r in range(NT)]],
}
NB_SET = 12
QK_SET = 8
BANK_FOX = 0
BANK_FOX_OUT = BANK_FOX + 2 * NB_SET
BANK_MLP = [BANK_FOX_OUT + 8, 0]
CHUNKS = DFF // D
BANK_DIL = BANK_MLP[0] + 16 * CHUNKS
BANK_DIL_OUT = BANK_DIL + 6 * NB_SET
BANK_MLP[1] = BANK_DIL_OUT + 8
N_BANKS = BANK_MLP[1] + 16 * CHUNKS


def set_bank0(s):
    return BANK_FOX + NB_SET * s if s < 2 else BANK_DIL + NB_SET * (s - 2)


def ticks_of(s):
    banks = SCORE_BANKS[SETS[s][0]]
    return [(h, i, i == len(banks) - 1) for h in range(HS) for i in range(len(banks))]


TICK0 = [0]
for _s in range(len(SETS)):
    TICK0.append(TICK0[-1] + len(ticks_of(_s)))


def ticks_of_step(attend):
    return len(ticks_of(attend)) + 4 if attend is not None else 1


def terms_of_tick(a, n):
    total = NB_SET * 3 * KT
    return range(a * total // n, (a + 1) * total // n)


def banks_of_tick(a, n):
    return [t // (3 * KT) for t in terms_of_tick(a, n) if t % (3 * KT) == 3 * KT - 1]


def head_cols(h):
    return slice((h % 2) * VC, (h % 2) * VC + VC)


def value_cols(h):
    return slice(1 + (h % 2) * HD, 1 + (h % 2) * HD + HD)


def own_values(h):
    return slice(1 - h % 2, 1 - h % 2 + HD)


def own_one(h):
    return (h % 2) * HD


STEPS_FOX = [(0, None), (1, 0), (None, 1)]
STEPS_DIL = [(2, None), (3, 2), (4, 3), (5, 4), (6, 5), (7, 6), (None, 7)]


def trunk(nc, x, positions, fox_norm, fox_w_in, fox_b_f, fox_q_gain, fox_k_gain, fox_w_out,
          dil_norm, dil_w_in, dil_q_gain, dil_k_gain, dil_w_out, mlp_norm, mlp_w1, mlp_w2, out):
    ctx = ExitStack()
    with ctx:
        def sb(name, shape, dt=F32, where=ctx):
            return where.enter_context(nc.sbuf_tensor(name, shape, dt))

        def sem(name):
            return ctx.enter_context(nc.semaphore(name))

        act_h = sb("act_h", [P, KT, S], F32R)
        act_l = sb("act_l", [P, KT, S], F32R)
        w_raw = sb("w_raw", [P, RAW, 2, 512])
        w_h = sb("w_h", [P, WR, 2, 512], F32R)
        w_l = sb("w_l", [P, WR, 2, 512], F32R)
        with ExitStack() as once:
            qT = [sb(f"qT{i}", [P, HS // 2, S], F32, once) for i in range(2)]
            kT = [sb(f"kT{i}", [P, HS // 2, S], F32, once) for i in range(2)]
        hid_h = sb("hid_h", [P, KT, S], F32R)
        hid_l = sb("hid_l", [P, KT, S], F32R)
        v_sb = [sb(f"v{i}", [P, NT, HS // 2, VP]) for i in range(2)]
        with ExitStack() as once:
            acc12 = sb("acc12", [P, NT, HS // 2, UP], F32, once)
            o_ring = sb("o_ring", [P, 2, NT, VC], F32, once)
            rt = sb("rt", [P, 2, HS, ROT], F32, once)
        x_sb = sb("x_sb", [P, NT, D])
        with ExitStack() as once:
            gw_raw = sb("gw_raw", [P, KT, NH], F32, once)
            gw_h = sb("gw_h", [P, KT, NH], F32R, once)
            gw_l = sb("gw_l", [P, KT, NH], F32R, once)
            z_g = sb("z_g", [P, NT, NH], F32, once)
            t_g = sb("t_g", [P, 2, NT, NH], F32, once)
            log_f = sb("log_f", [P, NT, NH], F32, once)
            upto_t = sb("upto_t", [P, P], F32, once)
            ones_t = sb("ones_t", [P, P], F32, once)
            b_f = sb("b_f", [P, NH], F32, once)
        o_sb = sb("o_sb", [P, NT, NH // 2, UP])
        sq = sb("sq", [P, 512])
        qn = sb("qn", [P, 2, 512])
        p_sb = sb("p_sb", [P, 2, 512])
        pT_sb = sb("pT_sb", [P, 2, 512])
        ident = sb("ident", [P, P])
        ident_b = sb("ident_b", [P, P], BF16)
        causal = sb("causal", [P, P], BF16)
        banded = sb("banded", [P, 256], BF16)
        residue = sb("residue", [P, P], BF16)
        pick = sb("pick", [P, NH], BF16)
        with ExitStack() as once:
            cos2 = sb("cos2", [P, 2, NT, ROT], F32, once)
            sin2 = sb("sin2", [P, 2, NT, ROT], F32, once)
        c_parts = sb("c_parts", [P, S], BF16)
        gain_t = sb("gain_t", [P, 4, KT])
        hg = sb("hg", [P, 8])
        xss = sb("xss", [P, 5, NT])
        xrs = sb("xrs", [P, 5, NT])
        xaux = sb("xaux", [P, 5, NT])
        qss = sb("qss", [P, 2, HS])
        qrs = sb("qrs", [P, 2, HS])
        m_half = sb("m_half", [P, HS])
        negmax = sb("negmax", [P, 6, HS, NT])
        e_arg = sb("e_arg", [P, 4, 2, NT])
        e_fac = sb("e_fac", [P, 4, 2, NT])
        rden = sb("rden", [P, 2, NT])
        rot_g = sb("rot_g", [P, 6, ROT])
        tab_a = sb("tab_a", [P, 6, NT, ROT])
        tab_b = sb("tab_b", [P, 6, NT, ROT])
        pos_i = sb("pos_i", [P, 2, NT], I32)
        pos_f = sb("pos_f", [P, 2 * NT])
        freq = sb("freq", [P, HALF])
        ang = sb("ang", [P, 2 * NT, HALF])
        turns = sb("turns", [P, 2 * NT, HALF])
        sin_t = sb("sin_t", [P, 2 * NT, HALF])
        sinh_t = turns

        ps = [ctx.enter_context(nc.psum_tensor(f"ps{i}", [P, 512], F32)) for i in range(8)]
        ps_proj, ps_q, ps_s, ps_p, ps_o = ps[0:2], ps[2], ps[3:5], ps[5:7], ps[7]
        o_ps = ps_o[:, 0:NT * VC].rearrange("p (t c) -> p t c", c=VC)
        x_dram = nc.dram_tensor("x_kept", (S, D), F32, kind="Internal").ap()
        ss_dram = nc.dram_tensor("ss_kept", (S,), F32, kind="Internal").ap()
        acc_dram = nc.dram_tensor("acc_kept", (S, HS // 2 * UP), F32, kind="Internal").ap()

        raw_in = [sem(f"raw_in{i}") for i in range(RAW)]
        gain_in, ss_out, ss_in, cum_full = sem("gain_in"), sem("ss_out"), sem("ss_in"), sem("cum_full")
        small_in, hgain_in, gate_in, pos_in = sem("small_in"), sem("hgain_in"), sem("gate_in"), sem("pos_in")
        x_in = [sem(f"x_in{t}") for t in range(NT)]
        wh_done, wl_done = sem("wh_done"), sem("wl_done")
        proj_full = sem("proj_full")
        gwh_done, gwl_done, gate_full, softplus_done = sem("gwh_done"), sem("gwl_done"), sem("gate_full"), sem("softplus_done")
        ident_done, consts_done, pool_done, angle_done, sin_done = (
            sem("ident_done"), sem("consts_done"), sem("pool_done"), sem("angle_done"), sem("sin_done"))
        xss_done, xrs_done, prep_full, acth_done, actl_done = (
            sem("xss_done"), sem("xrs_done"), sem("prep_full"), sem("acth_done"), sem("actl_done"))
        sq_done, qss_done, qrs_done, qn_done, rope_done, qt_full, qt_done, v_done = (
            sem("sq_done"), sem("qss_done"), sem("qrs_done"), sem("qn_done"), sem("rope_done"), sem("qt_full"), sem("qt_done"), sem("v_done"))
        s_full, max_done, exp_done, pt_full, pt_done, pv_done, o_done = (
            sem("s_full"), sem("max_done"), sem("exp_done"), sem("pt_full"), sem("pt_done"), sem("pv_done"), sem("o_done"))
        earg_done, efac_done, merged, normed = sem("earg_done"), sem("efac_done"), sem("merged"), sem("normed")
        acc_out, acc_in, x_out, x_back = sem("acc_out"), sem("acc_in"), sem("x_out"), sem("x_back")
        relu_done, sqr_done, hidh_done, hidl_done, x_added = (
            sem("relu_done"), sem("sqr_done"), sem("hidh_done"), sem("hidl_done"), sem("x_added"))
        dve_own, pool_own, act_own, out_done = sem("dve_own"), sem("pool_own"), sem("act_own"), sem("out_done")

        def f(ap):
            return ap.bitcast(F32)

        def tok(act, k, tile, layout):
            if layout == 0:
                return act[:, k, tile * P:(tile + 1) * P]
            return act[:, k, :].rearrange("p (i r) -> p r i", r=NT)[:, tile, :]

        PREP_OF_NORM = [0, 2, 3, 5]
        X_ADDS = [0, 8, 8 + 8 * CHUNKS, 16 + 8 * CHUNKS]

        def x_ready(eng, norm, t):
            if norm == 0:
                eng.wait_ge(x_in[t], 16)
            else:
                eng.wait_ge(x_added, X_ADDS[norm] - (NT - 1) + t)

        def bank_kind(B):
            for s in range(len(SETS)):
                b = B - set_bank0(s)
                if 0 <= b < NB_SET:
                    return ("qk", QK_SET * s + b) if b < QK_SET else ("v", 4 * s + b - QK_SET)
            if BANK_FOX_OUT <= B < BANK_FOX_OUT + 8:
                return "x", B - BANK_FOX_OUT
            if BANK_DIL_OUT <= B < BANK_DIL_OUT + 8:
                return "x", 8 + 8 * CHUNKS + B - BANK_DIL_OUT
            layer = 0 if B < BANK_DIL else 1
            i, j = divmod(B - BANK_MLP[layer], 16)
            if j < 8:
                return "hid", 8 * CHUNKS * layer + 8 * i + j
            return "x", 8 + (8 * CHUNKS + 8) * layer + 8 * i + j - 8

        def unit_gain(u):
            if u < BANK_FOX_OUT:
                return 0
            if BANK_DIL <= u < BANK_DIL_OUT:
                return 2
            for layer in range(2):
                if BANK_MLP[layer] <= u < BANK_MLP[layer] + 16 * CHUNKS:
                    return 2 * layer + 1 if (u - BANK_MLP[layer]) % 16 < 8 else None
            return None

        def norm_slot(s):
            kind = SETS[s][0]
            return 0 if kind == "fox" else 2 if LAYOUT[kind] == 0 else 4

        def wait_bank_free(pe, B):
            if B >= 2:
                kind, n = bank_kind(B - 2)
                pe.wait_ge({"qk": qn_done, "v": v_done, "hid": sqr_done, "x": x_added}[kind], n + 1)

        block = ctx.enter_context(nc.Block())

        @block.sync
        def _(sp):
            def unit(u, u_more, src):
                if u >= RAW:
                    sp.wait_ge(wl_done, u_more + (u - RAW + 1))
                sp.dma_start(w_raw[:, u % RAW, :, :], src).then_inc(raw_in[u % RAW], 16)

            def group(u, u_more, w, row, col):
                for j in range(4):
                    unit(u + j, u_more, w[bass.ds(row + 2 * j * P, 2 * P), bass.ds(col, 512)]
                         .rearrange("(k p) n -> p k n", p=P))

            def set_groups(s):
                kind, half = SETS[s]
                w = fox_w_in[0] if kind == "fox" else dil_w_in[0]
                base = 0 if kind == "fox" else 3 * D * kind
                for n in range(3):
                    group(set_bank0(s) + 4 * n, 0, w, 0, base + n * D + half * HC)

            def mlp_groups(layer):
                with sp.Fori(0, CHUNKS) as i:
                    b = BANK_MLP[layer]
                    group(b, i * 16, mlp_w1[layer], 0, i * D)
                    group(b + 4, i * 16, mlp_w1[layer], 0, i * D + 512)
                    group(b + 8, i * 16, mlp_w2[layer], i * D, 0)
                    group(b + 12, i * 16, mlp_w2[layer], i * D, 512)

            set_groups(0)
            set_groups(1)
            for n in range(2):
                group(BANK_FOX_OUT + 4 * n, 0, fox_w_out[0], 0, 512 * n)
            mlp_groups(0)
            for s in range(2, 8):
                set_groups(s)
            for n in range(2):
                group(BANK_DIL_OUT + 4 * n, 0, dil_w_out[0], 0, 512 * n)
            mlp_groups(1)
            total = 16 + 16 * CHUNKS
            for t in range(NT):
                sp.wait_ge(x_added, total - (NT - 1) + t)
                sp.dma_start(out[0, t * P:(t + 1) * P, :], x_sb[:, t, :]).then_inc(out_done, 16)
            sp.wait_ge(out_done, 16 * NT)

        @block.tensor
        def _(pe):
            mm = nc.tensor.matmul

            def product(ps_out, k, term, lhs, rhs):
                i, j = [(0, 0), (1, 0), (0, 1)][term]
                return mm(ps_out, lhs[i], rhs[j], start=(k == 0 and term == 0), stop=(k == KT - 1 and term == 2))

            def weights_ready(B, k, more=0):
                if k % 2 == 0 and B % 4 == 0:
                    pe.wait_ge(wl_done, more + (B + k // 2 + 1))

            def token_bank(B, k, term, tile, layout=0):
                slot = (B // 4 * 4 + k // 2) % WR
                if term == 0:
                    weights_ready(B, k)
                    if k == 0:
                        wait_bank_free(pe, B)
                return product(ps_proj[B % 2][:, :], k, term, (tok(act_h, k, tile, layout), tok(act_l, k, tile, layout)),
                               (w_h[:, slot, k % 2, :], w_l[:, slot, k % 2, :]))

            def prepare(n, t):
                if n in PREP_OF_NORM:
                    x_ready(pe, PREP_OF_NORM.index(n), t)
                for half in range(2):
                    pc = 8 * n + 2 * t + half
                    if pc % 8 >= 2:
                        pe.wait_ge(actl_done, pc - 1)
                    for i in range(4):
                        c = 4 * half + i
                        src = x_sb[:, t, c * P:(c + 1) * P] if n in PREP_OF_NORM else o_sb[:, t, c, 1:1 + P]
                        last = nc.tensor.transpose(ps_p[pc % 2][:, i * P:(i + 1) * P], src, ident[:, :])
                    last.then_inc(prep_full, 1)

            def scores(s, a):
                kind, half = SETS[s]
                h, i, _ = ticks_of(s)[a - TICK0[s]]
                rows = slice(HD * (h % 2), HD * (h % 2) + HD)
                if a >= 2:
                    pe.wait_ge(exp_done, a - 1)
                col = 0
                for q, k0, nk in SCORE_BANKS[kind][i]:
                    n = nk * P
                    dst = ps_s[a % 2][:, col:col + n]
                    mask = (causal[:, :] if kind in ("fox", 1) else
                            banded[:, 256 - n:256] if kind == 0 else residue[:, :])
                    if kind == "fox":
                        hh = HS * half + h
                        mm(dst, pick[:, hh:hh + 1].broadcast_to([P, P]), c_parts[:, k0 * P:k0 * P + n], start=True, stop=False)
                        mm(ps_s[a % 2][:, col + n - P:col + n], ident_b[:, :], mask, start=False, stop=False)
                    else:
                        mm(dst, ident_b[:, :], mask, start=True, stop=False)
                    last = mm(dst, qT[s % 2][rows, h // 2, q * P:(q + 1) * P],
                              kT[s % 2][rows, h // 2, k0 * P:k0 * P + n], start=False, stop=True)
                    col += n
                last.then_inc(s_full, 1)

            def width(s, a):
                return sum(nk for _, _, nk in SCORE_BANKS[SETS[s][0]][ticks_of(s)[a - TICK0[s]][1]])

            def turn_probs(s, a):
                pe.wait_ge(exp_done, a + 1)
                if a >= 2:
                    pe.wait_ge(pt_done, a - 1)
                for c in range(width(s, a)):
                    last = nc.tensor.transpose(ps_p[a % 2][:, c * P:(c + 1) * P], p_sb[:, a % 2, c * P:(c + 1) * P], ident[:, :])
                last.then_inc(pt_full, 1)

            def values(s, a):
                h, i, _ = ticks_of(s)[a - TICK0[s]]
                pe.wait_ge(pt_done, a + 1)
                if i == 0 and HS * s + h > 0:
                    pe.wait_ge(o_done, HS * s + h)
                if a == TICK0[s]:
                    pe.wait_ge(v_done, 4 * (s + 1))
                c = 0
                for q, k0, nk in SCORE_BANKS[SETS[s][0]][i]:
                    for k in range(nk):
                        last = mm(o_ps[:, q, 0:VC], pT_sb[:, a % 2, c * P:(c + 1) * P], v_sb[s % 2][:, k0 + k, h // 2, head_cols(h)],
                                  start=(k == 0), stop=(k == nk - 1))
                        c += 1
                last.then_inc(pv_done, 1)

            def turn_qk(s, b):
                n = QK_SET * s + b
                pe.wait_ge(qn_done if s < 2 else rope_done, n + 1 if s < 2 else n - QK_SET * 2 + 1)
                if n >= 1:
                    pe.wait_ge(qt_done, n)
                for i in range(4):
                    last = nc.tensor.transpose(ps_q[:, i * P:(i + 1) * P], qn[:, n % 2, i * P:(i + 1) * P], ident[:, :])
                last.then_inc(qt_full, 1)

            def step(proj, attend):
                n = ticks_of_step(attend)
                for a in range(n):
                    if attend is not None:
                        t0, nt = TICK0[attend], len(ticks_of(attend))
                        if a == 0:
                            pe.wait_ge(qt_done, QK_SET * (attend + 1))
                        if a < nt:
                            scores(attend, t0 + a)
                        if 2 <= a <= nt + 1:
                            turn_probs(attend, t0 + a - 2)
                        if 3 <= a <= nt + 2:
                            values(attend, t0 + a - 3)
                    if proj is None:
                        continue
                    kind = SETS[proj][0]
                    for m in terms_of_tick(a, n):
                        b, k, term = m // (3 * KT), m // 3 % KT, m % 3
                        B = set_bank0(proj) + b
                        if term == 0 and k == 0 and b < 4 and proj in (0, 2):
                            if proj == 0:
                                if b == 0:
                                    prepare(0, 0)
                                if b < 3:
                                    prepare(0, b + 1)
                                pe.wait_ge(actl_done, 2 * (b + 1))
                            else:
                                pe.wait_ge(actl_done, 8 * 3 + 8)
                        last = token_bank(B, k, term, b % 4, 0 if kind == "fox" else LAYOUT[kind])
                        if k == KT - 1 and term == 2:
                            last.then_inc(proj_full, 1)
                            if 1 <= b <= QK_SET:
                                turn_qk(proj, b - 1)
                            if proj == 0:
                                forget_gates(b)

            def forget_gates(b):
                if b == 3:
                    pe.wait_ge(gwl_done, 1)
                    for t in range(NT):
                        for k in range(KT):
                            for term in range(3):
                                last = product(ps_o[:, t * NH:(t + 1) * NH], k, term, (tok(act_h, k, t, 0), tok(act_l, k, t, 0)),
                                               (gw_h[:, k, :], gw_l[:, k, :]))
                    last.then_inc(gate_full, 1)
                if b == 9:
                    pe.wait_ge(pool_done, 1)
                    pe.wait_ge(softplus_done, 3)
                    for t in range(NT):
                        for before in range(t + 1):
                            last = mm(ps_s[0][0:NH, t * P:(t + 1) * P], log_f[:, before, :],
                                      (upto_t if before == t else ones_t)[:, :], start=(before == 0), stop=(before == t))
                    last.then_inc(cum_full, 1)

            def out_projection(B0, prep):
                for b in range(8):
                    if b == 0:
                        prepare(prep, 0)
                    if b < 3:
                        prepare(prep, b + 1)
                    if b < NT:
                        pe.wait_ge(actl_done, 8 * prep + 2 * (b + 1))
                    for k in range(KT):
                        for term in range(3):
                            last = token_bank(B0 + b, k, term, b % 4)
                    last.then_inc(proj_full, 1)
                    if b >= 5:
                        prepare(prep + 1, b - 5)
                prepare(prep + 1, 3)

            def mlp(layer):
                B0 = BANK_MLP[layer]
                pe.wait_ge(actl_done, 8 * (2 if layer == 0 else 5) + 8)
                def chunk(i, final):
                    for b in range(16):
                        B = B0 + b
                        if b in (0, 1):
                            pe.wait_ge(x_added, i * 8 + X_ADDS[1 if layer == 0 else 3] - 1 + b)
                        elif b < 10:
                            pe.wait_ge(sqr_done, i * 8 + (8 * CHUNKS * layer + b - 1))
                        else:
                            pe.wait_ge(x_added, i * 8 + (X_ADDS[1 if layer == 0 else 3] + b - 9))
                        for k in range(KT):
                            slot = (B // 4 * 4 + k // 2) % WR
                            weights_ready(B, k, i * 16)
                            w = (w_h[:, slot, k % 2, :], w_l[:, slot, k % 2, :])
                            if b < 8:
                                c = slice((b % 4) * P, (b % 4 + 1) * P)
                                lhs, rhs = (w[0][:, c], w[1][:, c]), (act_h[:, k, :], act_l[:, k, :])
                            else:
                                if b == 8:
                                    pe.wait_ge(hidl_done, i * 8 + (8 * CHUNKS * layer + k + 1))
                                c = slice((b % 4) * P, (b % 4 + 1) * P)
                                lhs, rhs = (hid_h[:, k, c], hid_l[:, k, c]), w
                            for term in range(3):
                                last = product(ps_proj[B % 2][:, :], k, term, lhs, rhs)
                        last.then_inc(proj_full, 1)
                        if final and layer == 0 and b >= 13:
                            prepare(3, b - 13)

                with pe.Fori(0, CHUNKS - 1) as i:
                    chunk(i, False)
                chunk(CHUNKS - 1, True)
                if layer == 0:
                    prepare(3, 3)

            pe.wait_ge(ident_done, 1)
            for n, (proj, attend) in enumerate(STEPS_FOX):
                if n == 1:
                    pe.wait_ge(softplus_done, 4)
                step(proj, attend)
            pe.wait_ge(o_done, 2 * HS)
            out_projection(BANK_FOX_OUT, 1)
            mlp(0)
            pe.wait_ge(pool_done, 2)
            for proj, attend in STEPS_DIL:
                step(proj, attend)
            pe.wait_ge(normed, 2 * HS)
            out_projection(BANK_DIL_OUT, 4)
            mlp(1)

        @block.scalar
        def _(act):
            fn = nc.scalar.activation
            own = [0]

            def link(ins):
                own[0] += 1
                ins.then_inc(act_own, 1)
                act.wait_ge(act_own, own[0])

            def split_high(u, more=0, raws=0):
                act.wait_ge(raw_in[u % RAW], raws + 16 * (u // RAW + 1))
                if u // 4 >= 2:
                    act.wait_ge(proj_full, more + 4 * (u // 4 - 1))
                norm = unit_gain(u + more if isinstance(more, int) else u)
                if norm is None:
                    nc.scalar.copy(w_h[:, u % WR, :, :], w_raw[:, u % RAW, :, :]).then_inc(wh_done, 1)
                else:
                    for j in range(2):
                        k = u % 4 * 2 + j
                        last = fn(w_h[:, u % WR, j, :], w_raw[:, u % RAW, j, :], ACT.Copy, scale=gain_t[:, norm, k:k + 1])
                    last.then_inc(wh_done, 1)

            def norm_sums(norm):
                for t in range(NT):
                    n = 4 * norm + t
                    x_ready(act, norm, t)
                    if n > 0:
                        act.wait_ge(xss_done, n)
                    fn(pT_sb[:, :, :].rearrange("p a b -> p (a b)"), x_sb[:, t, :], ACT.Square,
                       accum_out=xss[:, norm, t:t + 1]).then_inc(xss_done, 1)

            def prepare(n, t):
                for half in range(2):
                    pc = 8 * n + 2 * t + half
                    act.wait_ge(prep_full, pc + 1)
                    nc.scalar.copy(act_h[:, 4 * half:4 * half + 4, t * P:(t + 1) * P],
                                   ps_p[pc % 2][:, :].rearrange("p (k t) -> p k t", k=4)).then_inc(acth_done, 1)

            def qk_evacuate(s, b):
                kind, _ = SETS[s]
                n = QK_SET * s + b
                if b == 0 and s >= 2:
                    act.wait_ge(pv_done, TICK0[s - 1])
                act.wait_ge(qt_full, n + 1)
                g = (0 if kind == "fox" else 2 + 2 * kind) + b // 4
                dst = (qT if b < 4 else kT)[s % 2][:, :, (b % 4) * P:(b % 4 + 1) * P]
                fn(dst, ps_q[:, :].rearrange("p (i t) -> p i t", i=4), ACT.Copy, scale=hg[:, g:g + 1]).then_inc(qt_done, 1)

            def bank_event(s, b):
                B = set_bank0(s) + b
                split_high(B + 4)
                act.wait_ge(proj_full, B + 1)
                src = ps_proj[B % 2][:, :]
                if b < QK_SET:
                    n = QK_SET * s + b
                    if n >= 1:
                        act.wait_ge(qss_done, n)
                    fn(sq[:, :], src, ACT.Square).then_inc(sq_done, 1)
                else:
                    if b == QK_SET and s >= 2:
                        act.wait_ge(pv_done, TICK0[s - 1])
                    if b == QK_SET and s in (0, 2):
                        act.wait_ge(xrs_done, 1 + s)
                    t = b - QK_SET
                    fn(v_sb[s % 2][:, t, :, 1:1 + P], src.rearrange("p (h d) -> p h d", d=P), ACT.Copy,
                       scale=xrs[:, norm_slot(s), t:t + 1]).then_inc(v_done, 1)
                if 1 <= b <= QK_SET:
                    qk_evacuate(s, b - 1)

            merges = [0]

            def probs(s, a):
                kind, half = SETS[s]
                h, i, last_bank = ticks_of(s)[a - TICK0[s]]
                act.wait_ge(max_done, a + 1)
                if a >= 2:
                    act.wait_ge(pt_full, a - 1)
                col = 0
                for q, _, nk in SCORE_BANKS[kind][i]:
                    c = slice(col, col + nk * P)
                    last = fn(p_sb[:, a % 2, c], ps_s[a % 2][:, c], ACT.Exp, bias=negmax[:, s % 6, h, q:q + 1])
                    col += nk * P
                last.then_inc(exp_done, 1)
                if kind in (2, 0) and last_bank:
                    m = merges[0]
                    act.wait_ge(earg_done, m + 1)
                    if m >= 4:
                        act.wait_ge(merged, m - 3)
                    fn(e_fac[:, m % 4, :, :], e_arg[:, m % 4, :, :], ACT.Exp).then_inc(efac_done, 1)
                    merges[0] += 1

            def step(proj, attend):
                n = ticks_of_step(attend)
                for a in range(n):
                    if attend is not None and a < len(ticks_of(attend)):
                        probs(attend, TICK0[attend] + a)
                    if proj is not None:
                        for b in banks_of_tick(a, n):
                            if proj == 0 and b < 3:
                                prepare(0, b + 1)
                            bank_event(proj, b)
                            if proj == 0 and b == 5:
                                softplus()

            def softplus():
                act.wait_ge(softplus_done, 1)
                link(fn(t_g[:, 0, :, :], z_g[:, :, :], ACT.Abs))
                link(fn(t_g[:, 1, :, :], t_g[:, 0, :, :], ACT.Exp, scale=-1.0))
                fn(t_g[:, 0, :, :], t_g[:, 1, :, :], ACT.Ln, bias=1.0).then_inc(softplus_done, 1)

            def out_projection(B0, prep):
                prepare(prep, 0)
                for b in range(8):
                    if b < 3:
                        prepare(prep, b + 1)
                    split_high(B0 + b + 4)
                    if b >= 5:
                        prepare(prep + 1, b - 5)
                prepare(prep + 1, 3)

            def mlp(layer):
                B0, h0 = BANK_MLP[layer], 8 * CHUNKS * layer

                def hidden_high(i, j):
                    act.wait_ge(sqr_done, i * 8 + (h0 + j + 1))
                    nc.scalar.copy(hid_h[:, j, :], p_sb[:, j % 2, :]).then_inc(hidh_done, 1)

                def chunk(i, final):
                    for b in range(16):
                        B = B0 + b
                        if not (final and layer == 1 and b >= 12):
                            split_high(B + 4, i * 16, i * (16 * 16 // RAW))
                        if b < 8:
                            act.wait_ge(proj_full, i * 16 + (B + 1))
                            fn(qn[:, b % 2, :], ps_proj[B % 2][:, :], ACT.Relu).then_inc(relu_done, 1)
                        if 1 <= b <= 8:
                            hidden_high(i, b - 1)
                        if final and layer == 0 and b >= 13:
                            prepare(3, b - 13)

                with act.Fori(0, CHUNKS - 1) as i:
                    chunk(i, False)
                chunk(CHUNKS - 1, True)
                if layer == 0:
                    prepare(3, 3)

            norms = [fox_norm[0], mlp_norm[0], dil_norm[0], mlp_norm[1]]
            act.dma_start(x_sb[:, 0, :], x[0, 0:P, :]).then_inc(x_in[0], 16)
            act.dma_start(gain_t[:, 0, :], norms[0].rearrange("(k p) -> p k", p=P), allow_slow_non_contiguous=True).then_inc(gain_in, 16)
            for t in range(1, NT):
                act.dma_start(x_sb[:, t, :], x[0, t * P:(t + 1) * P, :]).then_inc(x_in[t], 16)
            act.dma_start(gw_raw[:, :, :], fox_w_in[0][:, 3 * D:3 * D + NH].rearrange("(k p) n -> p k n", p=P)).then_inc(gate_in, 16)
            act.dma_start(b_f[:, :], fox_b_f[0:1, :].partition_broadcast(P)).then_inc(gate_in, 16)
            for n in range(1, 4):
                act.dma_start(gain_t[:, n, :], norms[n].rearrange("(k p) -> p k", p=P), allow_slow_non_contiguous=True).then_inc(small_in, 16)
            prepare(0, 0)
            act.wait_ge(gain_in, 16)
            for u in range(4):
                split_high(u)
            norm_sums(0)
            act.wait_ge(gwh_done, 1)
            nc.scalar.copy(gw_h[:, :, :], gw_raw[:, :, :]).then_inc(gwh_done, 1)
            act.wait_ge(hgain_in, 1)
            step(*STEPS_FOX[0])
            act.wait_ge(softplus_done, 3)
            step(*STEPS_FOX[1])
            step(*STEPS_FOX[2])
            act.wait_ge(angle_done, 1)
            fn(sin_t[:, :, :], ang[:, :, :], ACT.Sin)
            fn(sinh_t[:, :, :], ang[:, :, :], ACT.Sin, scale=0.5).then_inc(sin_done, 1)
            act.wait_ge(small_in, 16 * 3)
            out_projection(BANK_FOX_OUT, 1)
            norm_sums(1)
            mlp(0)
            x_ready(act, 2, NT - 1)
            act.dma_start(x_dram.rearrange("(t p) d -> p t d", p=P), x_sb[:, :, :]).then_inc(x_out, 16)
            norm_sums(2)
            for proj, attend in STEPS_DIL:
                step(proj, attend)
            act.wait_ge(merged, 4 * HS)
            act.wait_ge(x_out, 16)
            act.dma_start(x_sb[:, :, :], x_dram.rearrange("(t p) d -> p t d", p=P)).then_inc(x_back, 16)
            out_projection(BANK_DIL_OUT, 4)
            norm_sums(3)
            mlp(1)

        @block.vector
        def _(dve):
            v = nc.vector
            own = [0]

            def link(ins):
                own[0] += 1
                ins.then_inc(dve_own, 1)
                dve.wait_ge(dve_own, own[0])

            def split_low(u, more=0):
                dve.wait_ge(wh_done, more + (u + 1))
                norm = unit_gain(u + more if isinstance(more, int) else u)
                if norm is None:
                    v.tensor_tensor(w_l[:, u % WR, :, :], w_raw[:, u % RAW, :, :], f(w_h[:, u % WR, :, :]), ALU.subtract).then_inc(wl_done, 1)
                else:
                    for j in range(2):
                        k = u % 4 * 2 + j
                        last = v.scalar_tensor_tensor(w_l[:, u % WR, j, :], w_raw[:, u % RAW, j, :], gain_t[:, norm, k:k + 1],
                                                      f(w_h[:, u % WR, j, :]), ALU.mult, ALU.subtract)
                    last.then_inc(wl_done, 1)

            def prepare(n, t):
                for half in range(2):
                    pc = 8 * n + 2 * t + half
                    dst = (slice(None), slice(4 * half, 4 * half + 4), slice(t * P, (t + 1) * P))
                    dve.wait_ge(acth_done, pc + 1)
                    v.tensor_tensor(act_l[dst], ps_p[pc % 2][:, :].rearrange("p (k t) -> p k t", k=4), f(act_h[dst]),
                                    ALU.subtract).then_inc(actl_done, 1)

            def bank_event(s, b):
                B = set_bank0(s) + b
                if b < QK_SET:
                    n = QK_SET * s + b
                    dve.wait_ge(sq_done, n + 1)
                    if n >= 2:
                        dve.wait_ge(qrs_done, n - 1)
                    v.tensor_reduce(qss[:, n % 2, :], sq[:, :].rearrange("p (h d) -> p h d", d=HD), AX, ALU.add).then_inc(qss_done, 1)
                split_low(B + 4)
                if b < QK_SET:
                    dve.wait_ge(qrs_done, n + 1)
                    if n >= 2:
                        dve.wait_ge(qt_full, n - 1)
                    v.tensor_tensor(qn[:, n % 2, :].rearrange("p (h d) -> p h d", d=HD),
                                    ps_proj[B % 2][:, :].rearrange("p (h d) -> p h d", d=HD),
                                    qrs[:, n % 2, :].unsqueeze(2).broadcast_to([P, HS, HD]), ALU.mult).then_inc(qn_done, 1)

            merges = [0]

            def maxima(s, a):
                kind, half = SETS[s]
                h, i, last_bank = ticks_of(s)[a - TICK0[s]]
                dve.wait_ge(s_full, a + 1)
                segs = SCORE_BANKS[kind][i]
                if len({nk for _, _, nk in segs}) == 1:
                    q0, nk = segs[0][0], segs[0][2]
                    last = v.tensor_reduce(negmax[:, s % 6, h, q0:q0 + len(segs)],
                                           ps_s[a % 2][:, 0:len(segs) * nk * P].rearrange("p (q k) -> p q k", k=nk * P),
                                           AX, ALU.max, negate=True)
                else:
                    col = 0
                    for q, _, nk in segs:
                        last = v.tensor_reduce(negmax[:, s % 6, h, q:q + 1], ps_s[a % 2][:, col:col + nk * P], AX, ALU.max, negate=True)
                        col += nk * P
                last.then_inc(max_done, 1)
                if kind in (2, 0) and last_bank:
                    m = merges[0]
                    dve.wait_ge(max_done, a + 1)
                    mine = negmax[:, s % 6, h, :]
                    if kind == 2:
                        other, both = negmax[:, (s - 1) % 6, h, :], acc12[:, :, h // 2, VP + h % 2]
                    else:
                        if h == 0:
                            dve.wait_ge(acc_in, 16 * (half + 1))
                        other = both = o_sb[:, :, (HS * half + h) // 2, VP + h % 2]
                    if kind == 2:
                        link(v.tensor_tensor(both, mine, other, ALU.min))
                        v.tensor_tensor(e_arg[:, m % 4, 0, :], both, other, ALU.subtract)
                        v.tensor_tensor(e_arg[:, m % 4, 1, :], both, mine, ALU.subtract).then_inc(earg_done, 1)
                    else:
                        link(v.tensor_tensor(rden[:, 0, :], mine, other, ALU.min))
                        v.tensor_tensor(e_arg[:, m % 4, 0, :], rden[:, 0, :], other, ALU.subtract)
                        v.tensor_tensor(e_arg[:, m % 4, 1, :], rden[:, 0, :], mine, ALU.subtract).then_inc(earg_done, 1)
                    merges[0] += 1

            def probs_back(s, a):
                w = P * sum(nk for _, _, nk in SCORE_BANKS[SETS[s][0]][ticks_of(s)[a - TICK0[s]][1]])
                dve.wait_ge(pt_full, a + 1)
                if a >= 2:
                    dve.wait_ge(pv_done, a - 1)
                v.tensor_copy(pT_sb[:, a % 2, 0:w], ps_p[a % 2][:, 0:w]).then_inc(pt_done, 1)

            evacuated = [0]

            def output(s, a):
                kind, half = SETS[s]
                h, _, last_bank = ticks_of(s)[a - TICK0[s]]
                if not last_bank:
                    return
                dve.wait_ge(pv_done, a + 1)
                if kind == "fox":
                    link(v.reciprocal(rden[:, 0, :], o_ps[:, :, own_one(h)]))
                    v.tensor_tensor(o_sb[:, :, (HS * half + h) // 2, value_cols(h)], o_ps[:, :, own_values(h)],
                                    rden[:, 0, :].unsqueeze(2).broadcast_to([P, NT, HD]), ALU.mult).then_inc(o_done, 1)
                elif kind == 1:
                    if h == 0:
                        if half == 0:
                            dve.wait_ge(x_out, 16)
                        else:
                            dve.wait_ge(acc_out, 16)
                    v.tensor_copy(acc12[:, :, h // 2, head_cols(h)], o_ps[:, :, 0:VC]).then_inc(o_done, 1)
                else:
                    m = evacuated[0]
                    if m >= 2:
                        dve.wait_ge(merged, m - 1)
                    v.tensor_copy(o_ring[:, m % 2, :, 0:VC], o_ps[:, :, 0:VC]).then_inc(o_done, 1)
                    evacuated[0] += 1

            def normalise(s, h):
                half = SETS[s][1]
                m = 2 * HS * half + HS + h
                dve.wait_ge(merged, m + 1)
                o = o_sb[:, :, (HS * half + h) // 2, head_cols(h)]
                link(v.reciprocal(rden[:, 1, :], o[:, :, own_one(h)]))
                v.tensor_tensor(o[:, :, own_values(h)], o[:, :, own_values(h)], rden[:, 1, :].unsqueeze(2).broadcast_to([P, NT, HD]), ALU.mult).then_inc(normed, 1)

            def step(proj, attend):
                n = ticks_of_step(attend)
                for a in range(n):
                    if attend is not None:
                        t0, nt, tl = TICK0[attend], len(ticks_of(attend)), ticks_of(attend)
                        if a < nt:
                            maxima(attend, t0 + a)
                        if 2 <= a <= nt + 1:
                            probs_back(attend, t0 + a - 2)
                        if 4 <= a and SETS[attend][0] == 0 and tl[a - 4][2]:
                            normalise(attend, tl[a - 4][0])
                        if 3 <= a <= nt + 2:
                            output(attend, t0 + a - 3)
                    if proj is not None:
                        for b in banks_of_tick(a, n):
                            if proj == 0 and b < 3:
                                prepare(0, b + 1)
                            bank_event(proj, b)
                            if proj == 0:
                                forget_gates(b)

            def forget_gates(b):
                if b == 4:
                    dve.wait_ge(gate_full, 1)
                    dve.wait_ge(xrs_done, 1)
                    for t in range(NT):
                        last = v.scalar_tensor_tensor(z_g[:, t, :], ps_o[:, t * NH:(t + 1) * NH], xrs[:, 0, t:t + 1], b_f[:, :],
                                                      ALU.mult, ALU.add)
                    last.then_inc(softplus_done, 1)
                if b == 6:
                    dve.wait_ge(softplus_done, 2)
                    v.scalar_tensor_tensor(log_f[:, :, :], z_g[:, :, :], 0.0, t_g[:, 0, :, :], ALU.min, ALU.subtract).then_inc(softplus_done, 1)
                if b == 9:
                    rem, c1 = t_g_rows, c_row
                    dve.wait_ge(cum_full, 1)
                    src = ps_s[0][0:NH, :]
                    for part in range(3):
                        link(v.tensor_copy(c1, src))
                        last = v.tensor_copy(c_parts[32 * part:32 * part + NH, :], c1)
                        if part < 2:
                            link(v.tensor_tensor(rem, src, c1, ALU.subtract))
                            src = rem
                    last.then_inc(softplus_done, 1)

            def x_add(B, t, half, count, more=0, norm=None):
                dve.wait_ge(proj_full, more + (B + 1))
                if count is not None:
                    dve.wait_ge(x_added, count)
                dst = x_sb[:, t, half * 512:(half + 1) * 512]
                if norm is None:
                    v.tensor_tensor(dst, ps_proj[B % 2][:, :], dst, ALU.add).then_inc(x_added, 1)
                else:
                    v.scalar_tensor_tensor(dst, ps_proj[B % 2][:, :], xaux[:, norm, t:t + 1], dst, ALU.mult, ALU.add).then_inc(x_added, 1)

            def out_projection(B0, prep):
                prepare(prep, 0)
                for b in range(8):
                    if b < 3:
                        prepare(prep, b + 1)
                    split_low(B0 + b + 4)
                    if b == 0 and prep == 4:
                        dve.wait_ge(x_back, 16)
                    x_add(B0 + b, b % 4, b // 4, None)
                    if b >= 5:
                        prepare(prep + 1, b - 5)
                prepare(prep + 1, 3)

            def mlp(layer):
                B0, h0 = BANK_MLP[layer], 8 * CHUNKS * layer

                def hidden_low(i, j):
                    dve.wait_ge(hidh_done, i * 8 + (h0 + j + 1))
                    v.tensor_tensor(hid_l[:, j, :], p_sb[:, j % 2, :], f(hid_h[:, j, :]), ALU.subtract).then_inc(hidl_done, 1)

                def chunk(i, final):
                    for b in range(16):
                        B = B0 + b
                        if b < 8:
                            dve.wait_ge(relu_done, i * 8 + (h0 + b + 1))
                            if b >= 2:
                                dve.wait_ge(hidl_done, i * 8 + (h0 + b - 1))
                            v.scalar_tensor_tensor(p_sb[:, b % 2, :], ps_proj[B % 2][:, :], 0.0, qn[:, b % 2, :],
                                                   ALU.max, ALU.mult).then_inc(sqr_done, 1)
                        if not (final and layer == 1 and b >= 12):
                            split_low(B + 4, i * 16)
                        if 1 <= b <= 8:
                            hidden_low(i, b - 1)
                        if b >= 8:
                            x_add(B, b % 4, (b - 8) // 4, i * 8 + (X_ADDS[1 if layer == 0 else 3] + b - 8), i * 16,
                                  2 * layer + 1)
                        if final and layer == 0 and b >= 13:
                            prepare(3, b - 13)

                dve.wait_ge(xrs_done, 2 * layer + 2)
                with dve.Fori(0, CHUNKS - 1) as i:
                    chunk(i, False)
                chunk(CHUNKS - 1, True)
                if layer == 0:
                    prepare(3, 3)

            t_g_rows = sq[0:NH, :]
            c_row = p_sb[0:NH, 1, 0:S // 2].bitcast(BF16)
            prepare(0, 0)
            for u in range(4):
                split_low(u)
            dve.wait_ge(gate_in, 32)
            v.tensor_tensor(gw_raw[:, :, :], gw_raw[:, :, :], gain_t[:, 0, :].unsqueeze(2).broadcast_to([P, KT, NH]),
                            ALU.mult).then_inc(gwh_done, 1)
            dve.wait_ge(gwh_done, 2)
            v.tensor_tensor(gw_l[:, :, :], gw_raw[:, :, :], f(gw_h[:, :, :]), ALU.subtract).then_inc(gwl_done, 1)
            for proj, attend in STEPS_FOX:
                step(proj, attend)
            out_projection(BANK_FOX_OUT, 1)
            mlp(0)
            for proj, attend in STEPS_DIL:
                step(proj, attend)
            out_projection(BANK_DIL_OUT, 4)
            mlp(1)

        @block.gpsimd
        def _(pool):
            g = nc.gpsimd
            own = [0]

            def link(ins):
                own[0] += 1
                ins.then_inc(pool_own, 1)
                pool.wait_ge(pool_own, own[0])

            def select(ap, pattern, base, cm, op, fill):
                link(g.affine_select(out=ap, in_=ap, compare_op=op, fill=fill, base=base, pattern=pattern, channel_multiplier=cm))

            def norm_scale(norm):
                pool.wait_ge(xss_done, 4 * (norm + 1))
                slots = [norm]
                if norm == 2:
                    pool.dma_start(ss_dram.rearrange("(t p) -> p t", p=P), xss[:, 2, :], allow_slow_non_contiguous=True).then_inc(ss_out, 16)
                    pool.wait_ge(ss_out, 16)
                    pool.dma_start(xss[:, 4, :], ss_dram.rearrange("(p r) -> p r", r=NT)).then_inc(ss_in, 16)
                    pool.wait_ge(ss_in, 16)
                    slots = [4, 2]
                for n in slots:
                    link(g.tensor_scalar(xss[:, n, :], xss[:, n, :], 1.0 / D, EPS, ALU.mult, ALU.add))
                    if norm % 2 == 0:
                        link(g.tensor_scalar(xaux[:, n, :], xss[:, n, :], HD * EPS, None, ALU.mult))
                    last = g.tensor_tensor(xrs[:, n, :], xss[:, n, :], m_half[:, 0:NT], ALU.pow)
                    if norm % 2 == 1:
                        link(last)
                        last = g.tensor_tensor(xaux[:, n, :], xrs[:, n, :], xrs[:, n, :], ALU.mult)
                last.then_inc(xrs_done, 1)

            def bank_event(s, b):
                if b >= QK_SET:
                    return
                kind, _ = SETS[s]
                n = QK_SET * s + b
                pool.wait_ge(qss_done, n + 1)
                link(g.tensor_scalar(qss[:, n % 2, :], qss[:, n % 2, :], xaux[:, norm_slot(s), b % 4:b % 4 + 1], None, ALU.add))
                g.tensor_tensor(qrs[:, n % 2, :], qss[:, n % 2, :], m_half[:, :], ALU.pow).then_inc(qrs_done, 1)
                if kind == "fox":
                    return
                pool.wait_ge(qn_done, n + 1)
                tab = 2 * kind + b // 4
                rot = qn[:, n % 2, :].rearrange("p (h d) -> p h d", d=HD)[:, :, 0:ROT]
                ta = tab_a[:, tab, b % 4, :].unsqueeze(1).broadcast_to([P, HS, ROT])
                tb = tab_b[:, tab, b % 4, :].unsqueeze(1).broadcast_to([P, HS, ROT])
                g.tensor_tensor(rt[:, 0, :, :], rot, ta, ALU.mult)
                g.tensor_tensor(rt[:, 1, :, 0:HALF], rot[:, :, HALF:ROT], tb[:, :, 0:HALF], ALU.mult)
                link(g.tensor_tensor(rt[:, 1, :, HALF:ROT], rot[:, :, 0:HALF], tb[:, :, HALF:ROT], ALU.mult))
                g.tensor_tensor(rot, rt[:, 0, :, :], rt[:, 1, :, :], ALU.add).then_inc(rope_done, 1)
                pool.wait_ge(rope_done, n - 2 * QK_SET + 1)

            merges = [0]

            def merge(s, a):
                kind, half = SETS[s]
                h, _, last_bank = ticks_of(s)[a - TICK0[s]]
                if kind not in (2, 0) or not last_bank:
                    return
                m = merges[0]
                acc = acc12[:, :, h // 2, head_cols(h)] if kind == 2 else o_sb[:, :, (HS * half + h) // 2, head_cols(h)]
                new = o_ring[:, m % 2, :, 0:VC]
                pool.wait_ge(efac_done, m + 1)
                pool.wait_ge(o_done, HS * s + h + 1)
                g.tensor_tensor(acc, acc, e_fac[:, m % 4, 0, :].unsqueeze(2).broadcast_to([P, NT, VC]), ALU.mult)
                link(g.tensor_tensor(new, new, e_fac[:, m % 4, 1, :].unsqueeze(2).broadcast_to([P, NT, VC]), ALU.mult))
                g.tensor_tensor(acc, acc, new, ALU.add).then_inc(merged, 1)
                merges[0] += 1

            def reorder(half):
                pool.wait_ge(merged, merges[0])
                if half:
                    pool.wait_ge(acc_in, 16)
                pool.dma_start(acc_dram.rearrange("(p r) c -> p r c", r=NT), acc12[:, :, :, :].rearrange("p r h c -> p r (h c)")).then_inc(acc_out, 16)
                pool.wait_ge(acc_out, 16 * (half + 1))
                pool.dma_start(o_sb[:, :, HS // 2 * half:HS // 2 * (half + 1), :].rearrange("p t h c -> p t (h c)"),
                               acc_dram.rearrange("(t p) c -> p t c", p=P)).then_inc(acc_in, 16)

            def step(proj, attend):
                n = ticks_of_step(attend)
                for a in range(n):
                    if attend is not None and 3 <= a <= len(ticks_of(attend)) + 2:
                        merge(attend, TICK0[attend] + a - 3)
                    if proj is not None:
                        for b in banks_of_tick(a, n):
                            bank_event(proj, b)
                if attend is not None and SETS[attend][0] == 2:
                    reorder(SETS[attend][1])

            link(g.memset(ident[:, :], 0.0))
            g.affine_select(out=ident[:, :], in_=ident[:, :], compare_op=ALU.not_equal, fill=1.0, base=0,
                            pattern=[[-1, P]], channel_multiplier=1).then_inc(ident_done, 1)
            pool.wait_ge(ident_done, 1)
            link(g.memset(m_half[:, :], -0.5))
            link(g.tensor_copy(ident_b[:, :], ident[:, :]))
            g.memset(hg[:, :], 1.0).then_inc(consts_done, 1)
            pool.wait_ge(consts_done, 1)
            for j, (gain, c) in enumerate([(fox_q_gain[0], 0), (fox_k_gain[0], 1)]
                                          + [(dil_q_gain[0, i], 2 + 2 * i) for i in range(3)]
                                          + [(dil_k_gain[0, i], 3 + 2 * i) for i in range(3)]):
                lo = 0 if c < 2 else ROT
                for r in (0, HD):
                    pool.dma_start(hg[r + lo:r + HD, c:c + 1], gain[lo:HD].rearrange("(d a) -> d a", a=1)).then_inc(pos_in, 16)
            for i in range(3):
                for n, gain in enumerate((dil_q_gain, dil_k_gain)):
                    pool.dma_start(rot_g[:, 2 * i + n, :], gain[0, i:i + 1, 0:ROT].partition_broadcast(P)).then_inc(pos_in, 16)
            pool.dma_start(pos_i[:, 1, :], positions[0].rearrange("(p r) -> p r", r=NT)).then_inc(pos_in, 16)
            pool.dma_start(pos_i[:, 0, :], positions[0].rearrange("(t p) -> p t", p=P), allow_slow_non_contiguous=True).then_inc(pos_in, 16)
            pool.wait_ge(pos_in, 16 * 24)
            kg = hg[:, :].rearrange("p (a b) -> p a b", b=2)[:, :, 1]
            g.tensor_scalar(kg, kg, float(HD) ** 0.5, None, ALU.mult).then_inc(hgain_in, 1)
            link(g.memset(causal[:, :], 0.0))
            select(causal[:, :], [[-1, P]], 0, 1, ALU.is_ge, NEG)
            link(g.memset(banded[:, :], 0.0))
            select(banded[:, 0:P], [[1, P]], 0, -1, ALU.is_ge, NEG)
            select(banded[:, P:2 * P], [[-1, P]], 0, 1, ALU.is_ge, NEG)
            link(g.memset(pick[:, :], 0.0))
            link(g.memset(c_parts[:, :], 0.0))
            for part in range(3):
                select(pick[32 * part:32 * part + NH, :], [[-1, NH]], 0, 1, ALU.not_equal, 1.0)
            for i in range(2):
                link(g.memset(v_sb[i][:, :, :, 0:VP:VP - 1], 1.0))
            link(g.memset(upto_t[:, :], -1.0))
            select(upto_t[:, :], [[1, P]], 0, -1, ALU.is_ge, 0.0)
            link(g.memset(ones_t[:, :], -1.0))
            norm_scale(0)
            pool.nop().then_inc(pool_done, 1)
            step(*STEPS_FOX[0])
            inv = np.float32(THETA) ** (-np.arange(HALF, dtype=np.float32) * np.float32(2.0) / np.float32(ROT))
            for j in range(HALF):
                g.memset(freq[:, j:j + 1], float(inv[j]))
            link(g.tensor_copy(pos_f[:, :], pos_i[:, :, :].rearrange("p a b -> p (a b)")))
            link(g.tensor_tensor(ang[:, :, :], pos_f[:, :].unsqueeze(2).broadcast_to([P, 2 * NT, HALF]),
                                 freq[:, :].unsqueeze(1).broadcast_to([P, 2 * NT, HALF]), ALU.mult))
            magic = float(1.5 * 2 ** 23)
            link(g.tensor_scalar(turns[:, :, :], ang[:, :, :], 1.0 / (2 * np.pi), magic, ALU.mult, ALU.add))
            link(g.tensor_scalar(turns[:, :, :], turns[:, :, :], magic, None, ALU.subtract))
            two_pi = 2 * np.pi
            c1 = 6.28125
            c2 = float(np.float32(round((two_pi - c1) * 2 ** 19) / 2 ** 19))
            c3 = float(np.float32(two_pi - c1 - c2))
            for c in (c1, c2, c3):
                link(g.tensor_scalar(sin_t[:, :, :], turns[:, :, :], c, None, ALU.mult))
                link(g.tensor_tensor(ang[:, :, :], ang[:, :, :], sin_t[:, :, :], ALU.subtract))
            pi_down = 3.1415925
            g.tensor_scalar(ang[:, :, :], ang[:, :, :], pi_down, -pi_down, ALU.min, ALU.max).then_inc(angle_done, 1)
            step(*STEPS_FOX[1])
            step(*STEPS_FOX[2])
            norm_scale(1)
            pool.wait_ge(sin_done, 1)
            link(g.tensor_tensor(sinh_t[:, :, :], sinh_t[:, :, :], sinh_t[:, :, :], ALU.mult))
            st = sin_t[:, :, :].rearrange("p (a t) j -> p a t j", a=2)
            ch = sinh_t[:, :, :].rearrange("p (a t) j -> p a t j", a=2)
            for lay in range(2):
                for hlf in range(2):
                    c = slice(hlf * HALF, (hlf + 1) * HALF)
                    link(g.tensor_scalar(cos2[:, lay, :, c], ch[:, lay, :, :], -2.0, 1.0, ALU.mult, ALU.add))
                    link(g.tensor_scalar(sin2[:, lay, :, c], st[:, lay, :, :], 2.0 * hlf - 1.0, None, ALU.mult))
            for tab in range(6):
                lay = LAYOUT[tab // 2]
                gn = rot_g[:, tab, :]
                link(g.tensor_tensor(tab_a[:, tab, :, :], cos2[:, lay, :, :], gn.unsqueeze(1).broadcast_to([P, NT, ROT]), ALU.mult))
                for hlf in range(2):
                    c = slice(hlf * HALF, (hlf + 1) * HALF)
                    o = slice((1 - hlf) * HALF, (2 - hlf) * HALF)
                    link(g.tensor_tensor(tab_b[:, tab, :, c], sin2[:, lay, :, c], gn[:, o].unsqueeze(1).broadcast_to([P, NT, HALF]), ALU.mult))
            link(g.memset(residue[:, :], NEG))
            for d in range(0, P, NT):
                select(residue[:, :], [[-1, P]], -d, 1, ALU.not_equal, 0.0)
            pool.nop().then_inc(pool_done, 1)
            norm_scale(2)
            pool.wait_ge(x_out, 16)
            for proj, attend in STEPS_DIL:
                step(proj, attend)
            norm_scale(3)


_INS = ["x", "positions", "fox_norm", "fox_w_in", "fox_b_f", "fox_q_gain", "fox_k_gain", "fox_w_out",
        "dil_norm", "dil_w_in", "dil_q_gain", "dil_k_gain", "dil_w_out", "mlp_norm", "mlp_w1", "mlp_w2"]


def kernel(**inputs):
    from concourse import bacc
    from concourse.bass_utils import run_bass_kernel_spmd

    nc = bacc.Bacc("TRN2", target_bir_lowering=False, num_devices=1)
    arrays, args = {}, []
    for name in _INS:
        a = np.ascontiguousarray(inputs[name])
        arrays[f"in_{name}"] = a
        args.append(nc.dram_tensor(f"in_{name}", a.shape, mybir.dt.from_np(a.dtype), kind="ExternalInput").ap())
    args.append(nc.dram_tensor("out_0", (1, S, D), F32, kind="ExternalOutput").ap())
    trunk(nc, *args)
    r = run_bass_kernel_spmd(nc, [arrays], core_ids=[0])
    return r.results[0]["out_0"]
```

```python
from contextlib import ExitStack
import numpy as np
import concourse.bass as bass
from concourse import mybir

F32 = mybir.dt.float32
F32R = mybir.dt.float32r
BF16 = mybir.dt.bfloat16
I32 = mybir.dt.int32
ALU = mybir.AluOpType
ACT = mybir.ActivationFunctionType
AX = mybir.AxisListType.X

P = 128
S, D, DFF = 512, 1024, 4096
HD = 64
NH = D // HD
NT = S // P
KT = D // P
EPS = 1e-6
NEG = -1e30
ROT = HD // 4
HALF = ROT // 2
THETA = 500000.0
HS = 8
HC = HS * HD
VC = HD + 1
VP = 2 * VC
UP = VP + 2
RAW = 2
WR = 8
LAYOUT = {0: 0, 1: 1, 2: 1}

SETS = [("fox", 0), ("fox", 1), (1, 0), (2, 0), (0, 0), (1, 1), (2, 1), (0, 1)]
SCORE_BANKS = {
    "fox": [[(0, 0, 1), (2, 0, 3)], [(1, 0, 2)], [(3, 0, 4)]],
    0: [[(0, 0, 1), (1, 0, 2)], [(2, 1, 2), (3, 2, 2)]],
    1: [[(r, r, 1) for r in range(NT)]],
    2: [[(r, r, 1) for r in range(NT)]],
}
NB_SET = 12
QK_SET = 8
BANK_FOX = 0
BANK_FOX_OUT = BANK_FOX + 2 * NB_SET
BANK_MLP = [BANK_FOX_OUT + 8, 0]
CHUNKS = DFF // D
BANK_DIL = BANK_MLP[0] + 16 * CHUNKS
BANK_DIL_OUT = BANK_DIL + 6 * NB_SET
BANK_MLP[1] = BANK_DIL_OUT + 8
N_BANKS = BANK_MLP[1] + 16 * CHUNKS


def set_bank0(s):
    return BANK_FOX + NB_SET * s if s < 2 else BANK_DIL + NB_SET * (s - 2)


def ticks_of(s):
    banks = SCORE_BANKS[SETS[s][0]]
    return [(h, i, i == len(banks) - 1) for h in range(HS) for i in range(len(banks))]


TICK0 = [0]
for _s in range(len(SETS)):
    TICK0.append(TICK0[-1] + len(ticks_of(_s)))


def ticks_of_step(attend):
    return len(ticks_of(attend)) + 4 if attend is not None else 1


CARRY = 2 * 3 * KT
CARRY_TICKS = 4


def terms_of_tick(proj, attend, a):
    total = NB_SET * 3 * KT
    if proj is None:
        a = min(a, CARRY_TICKS)
        first = total - CARRY
        return attend, range(first + a * CARRY // CARRY_TICKS, first + min(a + 1, CARRY_TICKS) * CARRY // CARRY_TICKS)
    if proj in (1, 7):
        total -= CARRY
    n = ticks_of_step(attend)
    return proj, range(a * total // n, (a + 1) * total // n)


def banks_of_tick(proj, attend, a):
    s, terms = terms_of_tick(proj, attend, a)
    return [(s, t // (3 * KT)) for t in terms if t % (3 * KT) == 3 * KT - 1]


def turns_of_tick(proj, attend, a):
    if proj is None or attend is None or a == 0:
        return []
    return [(s, b - 1) for s, b in banks_of_tick(proj, attend, a - 1) if 1 <= b <= QK_SET]


def mask_on_pe(s):
    return s == len(SETS) - 1


def head_cols(h):
    return slice((h % 2) * VC, (h % 2) * VC + VC)


def value_cols(h):
    return slice(1 + (h % 2) * HD, 1 + (h % 2) * HD + HD)


def own_values(h):
    return slice(1 - h % 2, 1 - h % 2 + HD)


def own_one(h):
    return (h % 2) * HD


def out_fill(a, attend):
    i = a - len(ticks_of(attend)) + 1
    return range(3 * i, 3 * i + 3) if 0 <= i < NT else range(0)


def out_early(a):
    return a // 2 if a % 2 == 1 and a < 2 * NT else None


STEPS_FOX = [(0, None), (1, 0), (None, 1)]
STEPS_DIL = [(2, None), (3, 2), (4, 3), (5, 4), (6, 5), (7, 6), (None, 7)]


def trunk(nc, x, positions, fox_norm, fox_w_in, fox_b_f, fox_q_gain, fox_k_gain, fox_w_out,
          dil_norm, dil_w_in, dil_q_gain, dil_k_gain, dil_w_out, mlp_norm, mlp_w1, mlp_w2, out):
    ctx = ExitStack()
    with ctx:
        def sb(name, shape, dt=F32, where=ctx):
            return where.enter_context(nc.sbuf_tensor(name, shape, dt))

        def sem(name):
            return ctx.enter_context(nc.semaphore(name))

        act_h = sb("act_h", [P, KT, S], F32R)
        act_l = sb("act_l", [P, KT, S], F32R)
        w_raw = sb("w_raw", [P, RAW, 2, 512])
        w_h = sb("w_h", [P, WR, 2, 512], F32R)
        w_l = sb("w_l", [P, WR, 2, 512], F32R)
        with ExitStack() as once:
            qT = [sb(f"qT{i}", [P, HS // 2, S], F32, once) for i in range(2)]
            kT = [sb(f"kT{i}", [P, HS // 2, S], F32, once) for i in range(2)]
        hid_h = sb("hid_h", [P, KT, S], F32R)
        hid_l = sb("hid_l", [P, KT, S], F32R)
        v_sb = [sb(f"v{i}", [P, NT, HS // 2, VP]) for i in range(2)]
        with ExitStack() as once:
            acc12 = sb("acc12", [P, NT, HS // 2, UP], F32, once)
            o_ring = sb("o_ring", [P, 2, NT, VC], F32, once)
            rt = sb("rt", [P, 2, HS, ROT], F32, once)
        x_sb = sb("x_sb", [P, NT, D])
        with ExitStack() as once:
            gw_raw = sb("gw_raw", [P, KT, NH], F32, once)
            gw_h = sb("gw_h", [P, KT, NH], F32R, once)
            gw_l = sb("gw_l", [P, KT, NH], F32R, once)
            z_g = sb("z_g", [P, NT, NH], F32, once)
            t_g = sb("t_g", [P, 2, NT, NH], F32, once)
            log_f = sb("log_f", [P, NT, NH], F32, once)
            upto_t = sb("upto_t", [P, P], F32, once)
            ones_t = sb("ones_t", [P, P], F32, once)
            b_f = sb("b_f", [P, NH], F32, once)
        o_sb = sb("o_sb", [P, NT, NH // 2, UP])
        sq = sb("sq", [P, 512])
        qn = sb("qn", [P, 2, 512])
        p_sb = sb("p_sb", [P, 2, 512])
        pT_sb = sb("pT_sb", [P, 2, 512])
        ident = sb("ident", [P, P])
        ident_b = sb("ident_b", [P, P], BF16)
        causal = sb("causal", [P, P], BF16)
        banded = sb("banded", [P, 256], BF16)
        residue = sb("residue", [P, P], BF16)
        pick = sb("pick", [P, NH], BF16)
        with ExitStack() as once:
            cos2 = sb("cos2", [P, 2, NT, ROT], F32, once)
            sin2 = sb("sin2", [P, 2, NT, ROT], F32, once)
        c_parts = sb("c_parts", [P, S], BF16)
        gain_t = sb("gain_t", [P, 4, KT])
        hg = sb("hg", [P, 8])
        quad = sb("quad", [P, P // NT])
        place = sb("place", [P, NT])
        xss = sb("xss", [P, 5, NT])
        xrs = sb("xrs", [P, 5, NT])
        xaux = sb("xaux", [P, 5, NT])
        qss = sb("qss", [P, 2, HS])
        qrs = sb("qrs", [P, 2, HS])
        m_half = sb("m_half", [P, HS])
        negmax = sb("negmax", [P, 6, HS, NT])
        e_arg = sb("e_arg", [P, 4, 2, NT])
        e_fac = sb("e_fac", [P, 4, 2, NT])
        rden = sb("rden", [P, 2, NT])
        rot_g = sb("rot_g", [P, 6, ROT])
        tab_a = sb("tab_a", [P, 6, NT, ROT])
        tab_b = sb("tab_b", [P, 6, NT, ROT])
        pos_i = sb("pos_i", [P, 2, NT], I32)
        pos_f = sb("pos_f", [P, 2 * NT])
        freq = sb("freq", [P, HALF])
        ang = sb("ang", [P, 2 * NT, HALF])
        turns = sb("turns", [P, 2 * NT, HALF])
        sin_t = sb("sin_t", [P, 2 * NT, HALF])
        sinh_t = turns

        ps = [ctx.enter_context(nc.psum_tensor(f"ps{i}", [P, 512], F32)) for i in range(8)]
        ps_proj, ps_q, ps_s, ps_p, ps_o = ps[0:2], ps[2], ps[3:5], ps[5:7], ps[7]
        o_ps = ps_o[:, 0:NT * VC].rearrange("p (t c) -> p t c", c=VC)
        x_dram = nc.dram_tensor("x_kept", (S, D), F32, kind="Internal").ap()
        acc_dram = nc.dram_tensor("acc_kept", (S, HS // 2 * UP), F32, kind="Internal").ap()

        def f(ap):
            return ap.bitcast(F32)

        def raw(u):
            return kT[0][:, 2 * (u - RAW):2 * (u - RAW) + 2, :] if RAW <= u < 4 else w_raw[:, u % RAW, :, :]

        spread = p_sb[:, 0, 0:P]
        g_rows = p_sb[0:NH, 0, :]

        raw_first = [sem(f"raw_first{u}") for u in range(4)]
        raw_in = [sem(f"raw_in{i}") for i in range(RAW)]
        gain_in, cum_full = sem("gain_in"), sem("cum_full")
        quad_done, spread_done, turned_full, turned_done = sem("quad_done"), sem("spread_done"), sem("turned_full"), sem("turned_done")
        small_in, fgain_in, hgain_in, gate_in, pos_in = sem("small_in"), sem("fgain_in"), sem("hgain_in"), sem("gate_in"), sem("pos_in")
        x_in, x_back = [sem(f"x_in{t}") for t in range(NT)], [sem(f"x_back{t}") for t in range(NT)]
        wh_done, wl_done = sem("wh_done"), sem("wl_done")
        proj_full = sem("proj_full")
        gwh_done, gwl_done, gate_full, gate_rows, softplus_done = (
            sem("gwh_done"), sem("gwl_done"), sem("gate_full"), sem("gate_rows"), sem("softplus_done"))
        ident_done, consts_done, pool_done, angle_done, sin_done = (
            sem("ident_done"), sem("consts_done"), sem("pool_done"), sem("angle_done"), sem("sin_done"))
        xss_done, xrs_done, prep_full, acth_done, actl_done = (
            sem("xss_done"), sem("xrs_done"), sem("prep_full"), sem("acth_done"), sem("actl_done"))
        sq_done, qss_done, qrs_done, qn_done, rope_done, qt_full, qt_done, v_done = (
            sem("sq_done"), sem("qss_done"), sem("qrs_done"), sem("qn_done"), sem("rope_done"), sem("qt_full"), sem("qt_done"), sem("v_done"))
        s_full, max_done, exp_done, pt_full, pt_done, pv_done, o_done = (
            sem("s_full"), sem("max_done"), sem("exp_done"), sem("pt_full"), sem("pt_done"), sem("pv_done"), sem("o_done"))
        earg_done, efac_done, merged, normed = sem("earg_done"), sem("efac_done"), sem("merged"), sem("normed")
        acc_out, acc_in, x_out = sem("acc_out"), sem("acc_in"), sem("x_out")
        relu_done, sqr_done, hidh_done, hidl_done, x_added = (
            sem("relu_done"), sem("sqr_done"), sem("hidh_done"), sem("hidl_done"), sem("x_added"))
        dve_own, pool_own, act_own, out_done = sem("dve_own"), sem("pool_own"), sem("act_own"), sem("out_done")

        def tok(act, k, tile, layout):
            if layout == 0:
                return act[:, k, tile * P:(tile + 1) * P]
            return act[:, k, :].rearrange("p (i r) -> p r i", r=NT)[:, tile, :]

        PREP_OF_NORM = [0, 2, 3, 5]
        PREP_OUT = [1, 4]
        X_ADDS = [0, 8, 8 + 8 * CHUNKS, 16 + 8 * CHUNKS]

        def x_ready(eng, norm, t, half=1):
            if norm == 0:
                eng.wait_ge(x_in[t], 16)
            else:
                eng.wait_ge(x_added, X_ADDS[norm] - 8 + 4 * half + t + 1)

        def prep_no(n, t, half):
            return 8 * n + (2 * t + half if n == 0 else 4 * half + t)

        def prep_bank(n, t, half):
            return ps_q if n in PREP_OUT and half == 0 else ps_p[prep_no(n, t, half) % 2]

        def prep_dst(n, half, t):
            i = (slice(None), slice(4 * half, 4 * half + 4), slice(t * P, (t + 1) * P))
            return (hid_h[i], hid_l[i]) if n in PREP_OUT else (act_h[i], act_l[i])

        def bank_kind(B):
            for s in range(len(SETS)):
                b = B - set_bank0(s)
                if 0 <= b < NB_SET:
                    return ("qk", QK_SET * s + b) if b < QK_SET else ("v", 4 * s + b - QK_SET)
            if BANK_FOX_OUT <= B < BANK_FOX_OUT + 8:
                return "x", B - BANK_FOX_OUT
            if BANK_DIL_OUT <= B < BANK_DIL_OUT + 8:
                return "x", 8 + 8 * CHUNKS + B - BANK_DIL_OUT
            layer = 0 if B < BANK_DIL else 1
            i, j = divmod(B - BANK_MLP[layer], 16)
            if j < 8:
                return "hid", 8 * CHUNKS * layer + 8 * i + j
            return "x", 8 + (8 * CHUNKS + 8) * layer + 8 * i + j - 8

        def unit_gain(u):
            if u < BANK_FOX_OUT:
                return 0
            if BANK_DIL <= u < BANK_DIL_OUT:
                return 2
            for layer in range(2):
                if BANK_MLP[layer] <= u < BANK_MLP[layer] + 16 * CHUNKS:
                    return 2 * layer + 1 if (u - BANK_MLP[layer]) % 16 < 8 else None
            return None

        def norm_slot(s):
            kind = SETS[s][0]
            return 0 if kind == "fox" else 2 if LAYOUT[kind] == 0 else 4

        def wait_bank_free(pe, B):
            if B >= 2:
                kind, n = bank_kind(B - 2)
                pe.wait_ge({"qk": qn_done, "v": v_done, "hid": sqr_done, "x": x_added}[kind], n + 1)

        block = ctx.enter_context(nc.Block())

        @block.sync
        def _(sp):
            def unit(u, u_more, src):
                sp.wait_ge(wl_done, u_more + (u - RAW + 1) if u >= 4 + RAW else u - 4 + 1)
                sp.dma_start(raw(u), src).then_inc(raw_in[u % RAW], 16)

            def group(u, u_more, w, row, col, halfway=None):
                for j in range(4):
                    if j == 2 and halfway:
                        halfway()
                    unit(u + j, u_more, w[bass.ds(row + 2 * j * P, 2 * P), bass.ds(col, 512)]
                         .rearrange("(k p) n -> p k n", p=P))

            def set_groups(s, first=0):
                kind, half = SETS[s]
                w = fox_w_in[0] if kind == "fox" else dil_w_in[0]
                base = 0 if kind == "fox" else 3 * D * kind
                for n in range(first, 3):
                    group(set_bank0(s) + 4 * n, 0, w, 0, base + n * D + half * HC, (lambda: reorder(0)) if s == 5 and n == 1 else small_loads if s == 0 and n == 1 else None)

            def mlp_groups(layer):
                with sp.Fori(0, CHUNKS) as i:
                    b = BANK_MLP[layer]
                    group(b, i * 16, mlp_w1[layer], 0, i * D)
                    group(b + 4, i * 16, mlp_w1[layer], 0, i * D + 512)
                    group(b + 8, i * 16, mlp_w2[layer], i * D, 0)
                    group(b + 12, i * 16, mlp_w2[layer], i * D, 512)

            def reorder(half):
                sp.wait_ge(merged, HS * (2 * half + 1))
                if half:
                    sp.wait_ge(acc_in, 16)
                sp.dma_start(acc_dram.rearrange("(p r) c -> p r c", r=NT), acc12[:, :, :, :].rearrange("p r h c -> p r (h c)")).then_inc(acc_out, 16)
                sp.wait_ge(acc_out, 16 * (half + 1))
                sp.dma_start(o_sb[:, :, HS // 2 * half:HS // 2 * (half + 1), :].rearrange("p t h c -> p t (h c)"),
                               acc_dram.rearrange("(t p) c -> p t c", p=P)).then_inc(acc_in, 16)

            def gain_column(gain, c, lo, done):
                for r in (0, HD):
                    sp.dma_start(hg[r + lo:r + HD, c:c + 1], gain[lo:HD].rearrange("(d a) -> d a", a=1)).then_inc(done, 16)

            for what, n in (("x", 0), ("w", 0), ("w", 1), ("w", 2), ("x", 1), ("w", 3), ("x", 2), ("x", 3)):
                if what == "x":
                    sp.dma_start(x_sb[:, n, :], x[0, n * P:(n + 1) * P, :]).then_inc(x_in[n], 16)
                else:
                    sp.dma_start(raw(n), fox_w_in[0][2 * n * P:(2 * n + 2) * P, 0:512].rearrange("(k p) n -> p k n", p=P)).then_inc(raw_first[n], 16)
            sp.wait_ge(consts_done, 1)
            gain_column(fox_q_gain[0], 0, 0, fgain_in)
            gain_column(fox_k_gain[0], 1, 0, fgain_in)
            sp.dma_start(gw_raw[:, :, :], fox_w_in[0][:, 3 * D:3 * D + NH].rearrange("(k p) n -> p k n", p=P)).then_inc(gate_in, 16)
            sp.dma_start(b_f[:, :], fox_b_f[0:1, :].partition_broadcast(P)).then_inc(gate_in, 16)
            for n, gain in ((1, mlp_norm[0]), (2, dil_norm[0]), (3, mlp_norm[1])):
                sp.dma_start(gain_t[:, n, :], gain.rearrange("(k p) -> p k", p=P), allow_slow_non_contiguous=True).then_inc(small_in, 16)
            def small_loads():
                for i in range(3):
                    gain_column(dil_q_gain[0, i], 2 + 2 * i, ROT, pos_in)
                    gain_column(dil_k_gain[0, i], 3 + 2 * i, ROT, pos_in)
                    for n, gain in enumerate((dil_q_gain, dil_k_gain)):
                        sp.dma_start(rot_g[:, 2 * i + n, :], gain[0, i:i + 1, 0:ROT].partition_broadcast(P)).then_inc(pos_in, 16)
                sp.dma_start(pos_i[:, 1, :], positions[0].rearrange("(p r) -> p r", r=NT)).then_inc(pos_in, 16)
                sp.dma_start(pos_i[:, 0, :], positions[0].rearrange("(t p) -> p t", p=P), allow_slow_non_contiguous=True).then_inc(pos_in, 16)

            set_groups(0, 1)
            set_groups(1)
            for n in range(2):
                group(BANK_FOX_OUT + 4 * n, 0, fox_w_out[0], 0, 512 * n)
            mlp_groups(0)
            for s in range(2, 8):
                set_groups(s)
            for n in range(2):
                if n == 1:
                    reorder(1)
                group(BANK_DIL_OUT + 4 * n, 0, dil_w_out[0], 0, 512 * n)
            mlp_groups(1)
            total = 16 + 16 * CHUNKS
            for half in range(2):
                for t in range(NT):
                    sp.wait_ge(x_added, total - 8 + 4 * half + t + 1)
                    c = slice(half * 512, (half + 1) * 512)
                    sp.dma_start(out[0, t * P:(t + 1) * P, c], x_sb[:, t, c]).then_inc(out_done, 16)
            sp.wait_ge(out_done, 16 * 2 * NT)

        @block.tensor
        def _(pe):
            mm = nc.tensor.matmul

            def product(ps_out, k, term, lhs, rhs):
                i, j = [(0, 0), (1, 0), (0, 1)][term]
                return mm(ps_out, lhs[i], rhs[j], start=(k == 0 and term == 0), stop=(k == KT - 1 and term == 2))

            def weights_ready(B, k, more=0):
                if k % 2 == 0 and B % 4 == 0:
                    pe.wait_ge(wl_done, more + (B + k // 2 + 1))

            def token_bank(B, k, term, tile, layout=0, out=False):
                slot = (B // 4 * 4 + k // 2) % WR
                if term == 0:
                    weights_ready(B, k)
                    if k == 0:
                        wait_bank_free(pe, B)
                a_h, a_l = (hid_h, hid_l) if out else (act_h, act_l)
                return product(ps_proj[B % 2][:, :], k, term, (tok(a_h, k, tile, layout), tok(a_l, k, tile, layout)),
                               (w_h[:, slot, k % 2, :], w_l[:, slot, k % 2, :]))

            def prepare(n, half, t):
                pc, bank = prep_no(n, t, half), prep_bank(n, t, half)
                if n in PREP_OF_NORM:
                    x_ready(pe, PREP_OF_NORM.index(n), t, half)
                if bank is ps_q:
                    if t >= 1:
                        pe.wait_ge(actl_done, pc)
                elif pc % 8 >= (6 if n in PREP_OUT else 2):
                    pe.wait_ge(actl_done, pc - 1)
                for i in range(4):
                    c = 4 * half + i
                    src = x_sb[:, t, c * P:(c + 1) * P] if n in PREP_OF_NORM else o_sb[:, t, c, 1:1 + P]
                    last = nc.tensor.transpose(bank[:, i * P:(i + 1) * P], src, ident[:, :])
                last.then_inc(prep_full, 1)

            def prepared(n, half, t):
                pe.wait_ge(actl_done, prep_no(n, t, half) + 1)

            def scores(s, a):
                kind, half = SETS[s]
                h, i, _ = ticks_of(s)[a - TICK0[s]]
                rows = slice(HD * (h % 2), HD * (h % 2) + HD)
                if a >= 2:
                    pe.wait_ge(exp_done, a - 1)
                col = 0
                for q, k0, nk in SCORE_BANKS[kind][i]:
                    n = nk * P
                    dst = ps_s[a % 2][:, col:col + n]
                    if kind == "fox":
                        hh = HS * half + h
                        mm(dst, pick[:, hh:hh + 1].broadcast_to([P, P]), c_parts[:, k0 * P:k0 * P + n], start=True, stop=False)
                    elif mask_on_pe(s):
                        mm(dst, ident_b[:, :], banded[:, 256 - n:256], start=True, stop=False)
                    last = mm(dst, qT[s % 2][rows, h // 2, q * P:(q + 1) * P],
                              kT[s % 2][rows, h // 2, k0 * P:k0 * P + n], start=kind != "fox" and not mask_on_pe(s), stop=True)
                    col += n
                last.then_inc(s_full, 1)

            def width(s, a):
                return sum(nk for _, _, nk in SCORE_BANKS[SETS[s][0]][ticks_of(s)[a - TICK0[s]][1]])

            def turn_probs(s, a):
                pe.wait_ge(exp_done, a + 1)
                if a >= 2:
                    pe.wait_ge(pt_done, a - 1)
                for c in range(width(s, a)):
                    last = nc.tensor.transpose(ps_p[a % 2][:, c * P:(c + 1) * P], p_sb[:, a % 2, c * P:(c + 1) * P], ident[:, :])
                last.then_inc(pt_full, 1)

            def values(s, a):
                h, i, _ = ticks_of(s)[a - TICK0[s]]
                pe.wait_ge(pt_done, a + 1)
                if i == 0 and HS * s + h > 0:
                    pe.wait_ge(o_done, HS * s + h)
                if a <= TICK0[s] + 1:
                    pe.wait_ge(v_done, 4 * s + 3 + a - TICK0[s])
                c = 0
                for q, k0, nk in SCORE_BANKS[SETS[s][0]][i]:
                    for k in range(nk):
                        last = mm(o_ps[:, q, 0:VC], pT_sb[:, a % 2, c * P:(c + 1) * P], v_sb[s % 2][:, k0 + k, h // 2, head_cols(h)],
                                  start=(k == 0), stop=(k == nk - 1))
                        c += 1
                last.then_inc(pv_done, 1)

            def turn_qk(s, b):
                n = QK_SET * s + b
                pe.wait_ge(qn_done if s < 2 else rope_done, n + 1 if s < 2 else n - QK_SET * 2 + 1)
                if n >= 1:
                    pe.wait_ge(qt_done, n)
                for i in range(4):
                    last = nc.tensor.transpose(ps_q[:, i * P:(i + 1) * P], qn[:, n % 2, i * P:(i + 1) * P], ident[:, :])
                last.then_inc(qt_full, 1)

            def step(proj, attend):
                n = ticks_of_step(attend)
                for a in range(n):
                    if attend is not None:
                        t0, nt = TICK0[attend], len(ticks_of(attend))
                        if a == 0:
                            pe.wait_ge(qt_done, QK_SET * (attend + 1))
                        if a < nt:
                            scores(attend, t0 + a)
                        if 2 <= a <= nt + 1:
                            turn_probs(attend, t0 + a - 2)
                        if 3 <= a <= nt + 2:
                            values(attend, t0 + a - 3)
                    for s, b in turns_of_tick(proj, attend, a):
                        turn_qk(s, b)
                    if proj is None:
                        t = out_early(a)
                        if t is not None:
                            if t == 0:
                                pe.wait_ge(o_done if attend == 1 else normed, HS)
                            prepare(1 if attend == 1 else 4, 0, t)
                        for m in out_fill(a, attend):
                            if m == 0:
                                prepared(1 if attend == 1 else 4, 0, 0)
                            token_bank(BANK_FOX_OUT if attend == 1 else BANK_DIL_OUT, m // 3, m % 3, 0, 0, True)
                    s, terms = terms_of_tick(proj, attend, a)
                    kind = SETS[s][0]
                    for m in terms:
                        b, k, term = m // (3 * KT), m // 3 % KT, m % 3
                        B = set_bank0(s) + b
                        if s == 0 and term == 0 and b < NT:
                            if k == 0:
                                prepared(0, 0, b)
                            if k == KT // 2:
                                prepared(0, 1, b)
                            if k == (5 if b == 0 else 3) and b + 1 < NT:
                                prepare(0, 0, b + 1)
                                prepare(0, 1, b + 1)
                        if attend is None and k == 1 and term == 0 and 2 <= b <= QK_SET + 1:
                            turn_qk(s, b - 2)
                        if proj == 2 and b == 0 and term == 0:
                            if k == 0:
                                prepared(3, 0, NT - 1)
                            if k == 2:
                                prepare(3, 1, NT - 1)
                            if k == KT // 2:
                                prepared(3, 1, NT - 1)
                            if k == 5:
                                pe.wait_ge(quad_done, 1)
                                pe.wait_ge(spread_done, 1)
                                mm(ps_s[0][:, 0:NT], spread, place[:, :], start=True, stop=True).then_inc(turned_full, 1)
                        last = token_bank(B, k, term, b % 4, 0 if kind == "fox" else LAYOUT[kind])
                        if k == KT - 1 and term == 2:
                            last.then_inc(proj_full, 1)
                            if proj == 0:
                                forget_gates(b)

            def forget_gates(b):
                if b == 3:
                    pe.wait_ge(gwl_done, 1)
                    for k in range(KT):
                        for term in range(3):
                            last = product(ps_o[0:NH, :], k, term, (gw_h[:, k, :], gw_l[:, k, :]), (act_h[:, k, :], act_l[:, k, :]))
                    last.then_inc(gate_full, 1)
                if b == 5:
                    pe.wait_ge(gate_rows, 1)
                    for t in range(NT):
                        last = nc.tensor.transpose(ps_o[:, t * NH:(t + 1) * NH], g_rows[:, t * P:(t + 1) * P], ident[0:NH, 0:NH])
                    last.then_inc(gate_full, 1)
                if b == 10:
                    pe.wait_ge(pool_done, 1)
                    pe.wait_ge(softplus_done, 3)
                    for t in range(NT):
                        for before in range(t + 1):
                            last = mm(ps_s[0][0:NH, t * P:(t + 1) * P], log_f[:, before, :],
                                      (upto_t if before == t else ones_t)[:, :], start=(before == 0), stop=(before == t))
                    last.then_inc(cum_full, 1)

            def out_projection(B0, prep):
                def terms(b, first, end):
                    for m in range(first, end):
                        last = token_bank(B0 + b, m // 3, m % 3, b % NT, 0, True)
                    if end == 3 * KT:
                        last.then_inc(proj_full, 1)

                half = 3 * KT // 2
                prepared(prep, 0, 1)
                terms(1, 0, 8)
                if prep == 1:
                    pe.wait_ge(o_done, 2 * HS)
                else:
                    pe.wait_ge(normed, 2 * HS)
                prepare(prep, 1, 0)
                terms(1, 8, half)
                prepare(prep, 1, 1)
                for b in range(8):
                    if b < NT:
                        prepared(prep, 1, b)
                    terms(b, half if b < 2 else 0, 3 * KT)
                    if b < 2:
                        prepare(prep, 1, b + 2)
                    if 2 <= b <= 5:
                        prepare(prep + 1, 0, b - 2)
                    if b >= 5:
                        prepare(prep + 1, 1, b - 5)

            def mlp(layer):
                B0, n = BANK_MLP[layer], 2 if layer == 0 else 5
                x0 = X_ADDS[1 if layer == 0 else 3]

                def tile(i, b, k):
                    B = B0 + b
                    if k == 0:
                        if b in (0, 1, 16):
                            pe.wait_ge(x_added, i * 8 + (x0 - 1 + (b if b < 16 else 8)))
                        elif b < 10:
                            pe.wait_ge(sqr_done, i * 8 + (8 * CHUNKS * layer + b - 1))
                        else:
                            pe.wait_ge(x_added, i * 8 + (x0 + b - 9))
                    slot = (B // 4 * 4 + k // 2) % WR
                    weights_ready(B, k, i * 16)
                    w = (w_h[:, slot, k % 2, :], w_l[:, slot, k % 2, :])
                    c = slice((b % 4) * P, (b % 4 + 1) * P)
                    if b % 16 < 8:
                        lhs, rhs = (w[0][:, c], w[1][:, c]), (act_h[:, k, :], act_l[:, k, :])
                    else:
                        if b == 8:
                            pe.wait_ge(hidl_done, i * 8 + (8 * CHUNKS * layer + k + 1))
                        lhs, rhs = (hid_h[:, k, c], hid_l[:, k, c]), w
                    for term in range(3):
                        last = product(ps_proj[B % 2][:, :], k, term, lhs, rhs)
                    if k == KT - 1:
                        last.then_inc(proj_full, 1)

                def chunk(i, final):
                    for b in range(16):
                        ks = range(KT // 2, KT) if b == 0 else range(KT - 1) if b == 8 else range(1, KT) if b == 9 else range(KT)
                        for k in ks:
                            tile(i, b, k)
                        if b == 8:
                            tile(i, 9, 0)
                            tile(i, 8, KT - 1)
                        if final and layer == 0 and b >= 9:
                            prepare(3, 0 if b < 13 else 1, (b - 9) % NT)
                    if not final:
                        for k in range(KT // 2):
                            tile(i, 16, k)

                prepared(n, 0, NT - 1)
                for k in range(KT // 2):
                    if k == 2:
                        prepare(n, 1, NT - 1)
                    tile(0, 0, k)
                prepared(n, 1, NT - 1)
                with pe.Fori(0, CHUNKS - 1) as i:
                    chunk(i, False)
                chunk(CHUNKS - 1, True)

            pe.wait_ge(ident_done, 1)
            prepare(0, 0, 0)
            prepare(0, 1, 0)
            for n, (proj, attend) in enumerate(STEPS_FOX):
                if n == 1:
                    pe.wait_ge(softplus_done, 4)
                step(proj, attend)
            out_projection(BANK_FOX_OUT, 1)
            mlp(0)
            pe.wait_ge(pool_done, 2)
            for proj, attend in STEPS_DIL:
                step(proj, attend)
            out_projection(BANK_DIL_OUT, 4)
            mlp(1)

        @block.scalar
        def _(act):
            fn = nc.scalar.activation
            own = [0]

            def link(ins):
                own[0] += 1
                ins.then_inc(act_own, 1)
                act.wait_ge(act_own, own[0])

            def split_high(u, more=0, raws=0):
                if u < 4:
                    act.wait_ge(raw_first[u], 16)
                else:
                    act.wait_ge(raw_in[u % RAW], raws + 16 * ((u - 4) // RAW + 1))
                if u // 4 >= 2:
                    act.wait_ge(proj_full, more + 4 * (u // 4 - 1))
                norm = unit_gain(u + more if isinstance(more, int) else u)
                if norm is None:
                    nc.scalar.copy(w_h[:, u % WR, :, :], raw(u)).then_inc(wh_done, 1)
                else:
                    for j in range(2):
                        k = u % 4 * 2 + j
                        last = fn(w_h[:, u % WR, j, :], raw(u)[:, j, :], ACT.Copy, scale=gain_t[:, norm, k:k + 1])
                    last.then_inc(wh_done, 1)

            def norm_sum(norm, t):
                n = 4 * norm + t
                x_ready(act, norm, t)
                if n > 0:
                    act.wait_ge(xss_done, n)
                fn(pT_sb[:, :, :].rearrange("p a b -> p (a b)"), x_sb[:, t, :], ACT.Square,
                   accum_out=xss[:, norm, t:t + 1]).then_inc(xss_done, 1)

            def prepare(n, half, t):
                act.wait_ge(prep_full, prep_no(n, t, half) + 1)
                nc.scalar.copy(prep_dst(n, half, t)[0],
                               prep_bank(n, t, half)[:, :].rearrange("p (k t) -> p k t", k=4)).then_inc(acth_done, 1)

            def qk_evacuate(s, b):
                kind, _ = SETS[s]
                n = QK_SET * s + b
                if b == 0 and s >= 2:
                    act.wait_ge(pv_done, TICK0[s - 1])
                act.wait_ge(qt_full, n + 1)
                g = (0 if kind == "fox" else 2 + 2 * kind) + b // 4
                dst = (qT if b < 4 else kT)[s % 2][:, :, (b % 4) * P:(b % 4 + 1) * P]
                fn(dst, ps_q[:, :].rearrange("p (i t) -> p i t", i=4), ACT.Copy, scale=hg[:, g:g + 1]).then_inc(qt_done, 1)

            def bank_event(s, b, attend):
                B = set_bank0(s) + b
                split_high(B + 4)
                act.wait_ge(proj_full, B + 1)
                src = ps_proj[B % 2][:, :]
                if b < QK_SET:
                    n = QK_SET * s + b
                    if n >= 1:
                        act.wait_ge(qss_done, n)
                    fn(sq[:, :], src, ACT.Square).then_inc(sq_done, 1)
                else:
                    if b == QK_SET and s >= 2:
                        act.wait_ge(pv_done, TICK0[s - 1])
                    if b == QK_SET and s in (0, 2):
                        act.wait_ge(xrs_done, 1 + s)
                    t = b - QK_SET
                    fn(v_sb[s % 2][:, t, :, 1:1 + P], src.rearrange("p (h d) -> p h d", d=P), ACT.Copy,
                       scale=xrs[:, norm_slot(s), t:t + 1]).then_inc(v_done, 1)
                if attend is None and 1 <= b <= QK_SET:
                    if b == 1:
                        act.wait_ge(hgain_in, 1 + s // 2)
                    qk_evacuate(s, b - 1)

            merges = [0]

            def probs(s, a):
                kind, half = SETS[s]
                h, i, last_bank = ticks_of(s)[a - TICK0[s]]
                act.wait_ge(max_done, a + 1)
                if a >= 2:
                    act.wait_ge(pt_full, a - 1)
                col = 0
                for q, _, nk in SCORE_BANKS[kind][i]:
                    c = slice(col, col + nk * P)
                    last = fn(p_sb[:, a % 2, c], ps_s[a % 2][:, c], ACT.Exp, bias=negmax[:, s % 6, h, q:q + 1])
                    col += nk * P
                last.then_inc(exp_done, 1)

            def factors(s, a):
                kind, _ = SETS[s]
                if kind in (2, 0) and ticks_of(s)[a - TICK0[s]][2]:
                    m = merges[0]
                    act.wait_ge(earg_done, m + 1)
                    if m >= 4:
                        act.wait_ge(merged, m - 3)
                    fn(e_fac[:, m % 4, :, :], e_arg[:, m % 4, :, :], ACT.Exp).then_inc(efac_done, 1)
                    merges[0] += 1

            def step(proj, attend):
                n = ticks_of_step(attend)
                for a in range(n):
                    if attend is not None and a < len(ticks_of(attend)):
                        probs(attend, TICK0[attend] + a)
                    for s, b in turns_of_tick(proj, attend, a):
                        qk_evacuate(s, b)
                    if attend is not None and 2 <= a <= len(ticks_of(attend)) + 1:
                        factors(attend, TICK0[attend] + a - 2)
                    if proj is None:
                        if out_early(a) is not None:
                            prepare(1 if attend == 1 else 4, 0, out_early(a))
                    for s, b in banks_of_tick(proj, attend, a):
                        bank_event(s, b, attend)
                        if s == 0 and b < 2:
                            prepare(0, 0, b + 2)
                            prepare(0, 1, b + 2)
                        if proj == 0 and b == 1:
                            act.wait_ge(gwh_done, 1)
                            nc.scalar.copy(gw_h[:, :, :], gw_raw[:, :, :]).then_inc(gwh_done, 1)
                        if proj == 0 and b == 7:
                            softplus()

            def softplus():
                act.wait_ge(softplus_done, 1)
                link(fn(t_g[:, 0, :, :], z_g[:, :, :], ACT.Abs))
                link(fn(t_g[:, 1, :, :], t_g[:, 0, :, :], ACT.Exp, scale=-1.0))
                fn(t_g[:, 0, :, :], t_g[:, 1, :, :], ACT.Ln, bias=1.0).then_inc(softplus_done, 1)

            def out_projection(B0, prep):
                norm = PREP_OF_NORM.index(prep + 1)
                prepare(prep, 1, 0)
                prepare(prep, 1, 1)
                for b in range(8):
                    split_high(B0 + b + 4)
                    if b < 2:
                        prepare(prep, 1, b + 2)
                    if 2 <= b <= 5:
                        prepare(prep + 1, 0, b - 2)
                    if b >= 5:
                        prepare(prep + 1, 1, b - 5)
                        norm_sum(norm, b - 5)
                prepare(prep + 1, 1, 3)
                norm_sum(norm, 3)

            def mlp(layer):
                B0, h0 = BANK_MLP[layer], 8 * CHUNKS * layer

                def hidden_high(i, j):
                    act.wait_ge(sqr_done, i * 8 + (h0 + j + 1))
                    nc.scalar.copy(hid_h[:, j, :], p_sb[:, j % 2, :]).then_inc(hidh_done, 1)

                def chunk(i, final):
                    for b in range(16):
                        B = B0 + b
                        if not (final and layer == 1 and b >= 12):
                            split_high(B + 4, i * 16, i * (16 * 16 // RAW))
                        if b < 8:
                            act.wait_ge(proj_full, i * 16 + (B + 1))
                            fn(qn[:, b % 2, :], ps_proj[B % 2][:, :], ACT.Relu).then_inc(relu_done, 1)
                        if 1 <= b <= 8:
                            hidden_high(i, b - 1)
                        if final and layer == 0 and b >= 9:
                            prepare(3, 0 if b < 13 else 1, (b - 9) % NT)
                            if b >= 13:
                                keep(b - 13)

                def keep(t):
                    norm_sum(2, t)
                    act.dma_start(x_dram[t * P:(t + 1) * P, :], x_sb[:, t, :]).then_inc(x_out, 16)

                with act.Fori(0, CHUNKS - 1) as i:
                    chunk(i, False)
                chunk(CHUNKS - 1, True)
                if layer == 0:
                    prepare(3, 1, 3)
                    keep(3)

            act.dma_start(gain_t[:, 0, :], fox_norm[0].rearrange("(k p) -> p k", p=P), allow_slow_non_contiguous=True).then_inc(gain_in, 16)
            act.wait_ge(ident_done, 1)
            nc.scalar.copy(ident_b[:, :], ident[:, :])
            prepare(0, 0, 0)
            prepare(0, 1, 0)
            act.wait_ge(gain_in, 16)
            for u in range(4):
                split_high(u)
            for t in range(NT):
                norm_sum(0, t)
                if t == 1:
                    prepare(0, 0, 1)
                    prepare(0, 1, 1)
            step(*STEPS_FOX[0])
            act.wait_ge(softplus_done, 3)
            step(*STEPS_FOX[1])
            step(*STEPS_FOX[2])
            act.wait_ge(angle_done, 1)
            fn(sin_t[:, :, :], ang[:, :, :], ACT.Sin)
            fn(sinh_t[:, :, :], ang[:, :, :], ACT.Sin, scale=0.5).then_inc(sin_done, 1)
            act.wait_ge(small_in, 16 * 3)
            out_projection(BANK_FOX_OUT, 1)
            mlp(0)
            for proj, attend in STEPS_DIL:
                step(proj, attend)
            act.wait_ge(merged, 4 * HS)
            act.wait_ge(x_out, 16 * NT)
            for t in range(NT):
                act.dma_start(x_sb[:, t, :], x_dram[t * P:(t + 1) * P, :]).then_inc(x_back[t], 16)
            out_projection(BANK_DIL_OUT, 4)
            mlp(1)

        @block.vector
        def _(dve):
            v = nc.vector
            own = [0]

            def link(ins):
                own[0] += 1
                ins.then_inc(dve_own, 1)
                dve.wait_ge(dve_own, own[0])

            def split_low(u, more=0):
                dve.wait_ge(wh_done, more + (u + 1))
                norm = unit_gain(u + more if isinstance(more, int) else u)
                if norm is None:
                    v.tensor_tensor(w_l[:, u % WR, :, :], raw(u), f(w_h[:, u % WR, :, :]), ALU.subtract).then_inc(wl_done, 1)
                else:
                    for j in range(2):
                        k = u % 4 * 2 + j
                        last = v.scalar_tensor_tensor(w_l[:, u % WR, j, :], raw(u)[:, j, :], gain_t[:, norm, k:k + 1],
                                                      f(w_h[:, u % WR, j, :]), ALU.mult, ALU.subtract)
                    last.then_inc(wl_done, 1)

            def prepare(n, half, t):
                high, low = prep_dst(n, half, t)
                dve.wait_ge(acth_done, prep_no(n, t, half) + 1)
                v.tensor_tensor(low, prep_bank(n, t, half)[:, :].rearrange("p (k t) -> p k t", k=4), f(high),
                                ALU.subtract).then_inc(actl_done, 1)

            def norm_turned():
                dve.wait_ge(turned_full, 1)
                v.tensor_copy(xss[:, 4, :], ps_s[0][:, 0:NT])
                v.tensor_scalar(xaux[:, 4, :], ps_s[0][:, 0:NT], HD * EPS, None, ALU.mult).then_inc(turned_done, 1)

            def bank_event(s, b, attend):
                B = set_bank0(s) + b
                if s == 2 and b == 0:
                    norm_turned()
                if b < QK_SET:
                    n = QK_SET * s + b
                    dve.wait_ge(sq_done, n + 1)
                    if n >= 2:
                        dve.wait_ge(qrs_done, n - 1)
                    v.tensor_reduce(qss[:, n % 2, :], sq[:, :].rearrange("p (h d) -> p h d", d=HD), AX, ALU.add).then_inc(qss_done, 1)
                split_low(B + 4)
                if s == 0 and b < 2:
                    prepare(0, 0, b + 2)
                    prepare(0, 1, b + 2)
                if attend is None:
                    norm_qk(s, b)

            def norm_qk(s, b):
                B, n = set_bank0(s) + b, QK_SET * s + b
                if b < QK_SET:
                    dve.wait_ge(qrs_done, n + 1)
                    if n >= 2:
                        dve.wait_ge(qt_full, n - 1)
                    v.tensor_tensor(qn[:, n % 2, :].rearrange("p (h d) -> p h d", d=HD),
                                    ps_proj[B % 2][:, :].rearrange("p (h d) -> p h d", d=HD),
                                    qrs[:, n % 2, :].unsqueeze(2).broadcast_to([P, HS, HD]), ALU.mult).then_inc(qn_done, 1)

            merges = [0]

            def maxima(s, a):
                kind, half = SETS[s]
                h, i, last_bank = ticks_of(s)[a - TICK0[s]]
                dve.wait_ge(s_full, a + 1)
                segs = SCORE_BANKS[kind][i]
                if kind == "fox":
                    end = 0
                    for _, _, nk in segs:
                        end += nk * P
                        own_tile = ps_s[a % 2][:, end - P:end]
                        last = v.tensor_tensor(own_tile, own_tile, causal[:, :], ALU.add)
                    link(last)
                elif not mask_on_pe(s):
                    col = 0
                    if kind == 0 and segs[0][2] == 1:
                        v.tensor_tensor(ps_s[a % 2][:, 0:P], ps_s[a % 2][:, 0:P], causal[:, :], ALU.add)
                        col = P
                    mask = banded if kind == 0 else causal if kind == 1 else residue
                    m = mask.shape[1]
                    many = (len(segs) * P if kind != 0 else (len(segs) - (col > 0)) * m) // m
                    rest = ps_s[a % 2][:, col:col + many * m].rearrange("p (q k) -> p q k", k=m)
                    link(v.tensor_tensor(rest, rest, mask[:, :].unsqueeze(1).broadcast_to([P, many, m]), ALU.add))
                if len({nk for _, _, nk in segs}) == 1:
                    q0, nk = segs[0][0], segs[0][2]
                    last = v.tensor_reduce(negmax[:, s % 6, h, q0:q0 + len(segs)],
                                           ps_s[a % 2][:, 0:len(segs) * nk * P].rearrange("p (q k) -> p q k", k=nk * P),
                                           AX, ALU.max, negate=True)
                else:
                    col = 0
                    for q, _, nk in segs:
                        last = v.tensor_reduce(negmax[:, s % 6, h, q:q + 1], ps_s[a % 2][:, col:col + nk * P], AX, ALU.max, negate=True)
                        col += nk * P
                last.then_inc(max_done, 1)

            def factor_args(s, a):
                kind, half = SETS[s]
                h, _, last_bank = ticks_of(s)[a - TICK0[s]]
                if kind in (2, 0) and last_bank:
                    m = merges[0]
                    dve.wait_ge(max_done, a + 1)
                    mine = negmax[:, s % 6, h, :]
                    if kind == 2:
                        other, both = negmax[:, (s - 1) % 6, h, :], acc12[:, :, h // 2, VP + h % 2]
                    else:
                        if h == 0:
                            dve.wait_ge(acc_in, 16 * (half + 1))
                        other = both = o_sb[:, :, (HS * half + h) // 2, VP + h % 2]
                    if kind == 2:
                        link(v.tensor_tensor(both, mine, other, ALU.min))
                        v.tensor_tensor(e_arg[:, m % 4, 0, :], both, other, ALU.subtract)
                        v.tensor_tensor(e_arg[:, m % 4, 1, :], both, mine, ALU.subtract).then_inc(earg_done, 1)
                    else:
                        link(v.tensor_tensor(rden[:, 0, :], mine, other, ALU.min))
                        v.tensor_tensor(e_arg[:, m % 4, 0, :], rden[:, 0, :], other, ALU.subtract)
                        v.tensor_tensor(e_arg[:, m % 4, 1, :], rden[:, 0, :], mine, ALU.subtract).then_inc(earg_done, 1)
                    merges[0] += 1

            def probs_back(s, a):
                w = P * sum(nk for _, _, nk in SCORE_BANKS[SETS[s][0]][ticks_of(s)[a - TICK0[s]][1]])
                dve.wait_ge(pt_full, a + 1)
                if a >= 2:
                    dve.wait_ge(pv_done, a - 1)
                v.tensor_copy(pT_sb[:, a % 2, 0:w], ps_p[a % 2][:, 0:w]).then_inc(pt_done, 1)

            evacuated = [0]

            def output(s, a):
                kind, half = SETS[s]
                h, _, last_bank = ticks_of(s)[a - TICK0[s]]
                if not last_bank:
                    return
                dve.wait_ge(pv_done, a + 1)
                if kind == "fox":
                    link(v.reciprocal(rden[:, 0, :], o_ps[:, :, own_one(h)]))
                    v.tensor_tensor(o_sb[:, :, (HS * half + h) // 2, value_cols(h)], o_ps[:, :, own_values(h)],
                                    rden[:, 0, :].unsqueeze(2).broadcast_to([P, NT, HD]), ALU.mult).then_inc(o_done, 1)
                elif kind == 1:
                    if h == 0:
                        if half == 0:
                            dve.wait_ge(x_out, 16 * NT)
                        else:
                            dve.wait_ge(acc_out, 16)
                    v.tensor_copy(acc12[:, :, h // 2, head_cols(h)], o_ps[:, :, 0:VC]).then_inc(o_done, 1)
                else:
                    m = evacuated[0]
                    if m >= 2:
                        dve.wait_ge(merged, m - 1)
                    v.tensor_copy(o_ring[:, m % 2, :, 0:VC], o_ps[:, :, 0:VC]).then_inc(o_done, 1)
                    evacuated[0] += 1

            def normalise(s, h):
                half = SETS[s][1]
                m = 2 * HS * half + HS + h
                dve.wait_ge(merged, m + 1)
                o = o_sb[:, :, (HS * half + h) // 2, head_cols(h)]
                link(v.reciprocal(rden[:, 1, :], o[:, :, own_one(h)]))
                v.tensor_tensor(o[:, :, own_values(h)], o[:, :, own_values(h)], rden[:, 1, :].unsqueeze(2).broadcast_to([P, NT, HD]), ALU.mult).then_inc(normed, 1)

            def step(proj, attend):
                n = ticks_of_step(attend)
                for a in range(n):
                    if attend is not None:
                        t0, nt, tl = TICK0[attend], len(ticks_of(attend)), ticks_of(attend)
                        if a < nt:
                            maxima(attend, t0 + a)
                        if proj is not None and a > 0:
                            for s, b in banks_of_tick(proj, attend, a - 1):
                                norm_qk(s, b)
                        if 2 <= a <= nt + 1:
                            probs_back(attend, t0 + a - 2)
                            factor_args(attend, t0 + a - 2)
                        if 4 <= a and SETS[attend][0] == 0 and tl[a - 4][2]:
                            normalise(attend, tl[a - 4][0])
                        if 3 <= a <= nt + 2:
                            output(attend, t0 + a - 3)
                    if proj is None:
                        if out_early(a) is not None:
                            prepare(1 if attend == 1 else 4, 0, out_early(a))
                    for s, b in banks_of_tick(proj, attend, a):
                        bank_event(s, b, attend)
                        if proj == 0:
                            forget_gates(b)

            def forget_gates(b):
                if b == 0:
                    dve.wait_ge(gate_in, 32)
                    v.tensor_tensor(gw_raw[:, :, :], gw_raw[:, :, :], gain_t[:, 0, :].unsqueeze(2).broadcast_to([P, KT, NH]),
                                    ALU.mult).then_inc(gwh_done, 1)
                if b == 2:
                    dve.wait_ge(gwh_done, 2)
                    v.tensor_tensor(gw_l[:, :, :], gw_raw[:, :, :], f(gw_h[:, :, :]), ALU.subtract).then_inc(gwl_done, 1)
                if b == 4:
                    dve.wait_ge(gate_full, 1)
                    v.tensor_copy(g_rows, ps_o[0:NH, :]).then_inc(gate_rows, 1)
                if b == 6:
                    dve.wait_ge(gate_full, 2)
                    dve.wait_ge(xrs_done, 1)
                    for t in range(NT):
                        last = v.scalar_tensor_tensor(z_g[:, t, :], ps_o[:, t * NH:(t + 1) * NH], xrs[:, 0, t:t + 1], b_f[:, :],
                                                      ALU.mult, ALU.add)
                    last.then_inc(softplus_done, 1)
                if b == 8:
                    dve.wait_ge(softplus_done, 2)
                    v.scalar_tensor_tensor(log_f[:, :, :], z_g[:, :, :], 0.0, t_g[:, 0, :, :], ALU.min, ALU.subtract).then_inc(softplus_done, 1)
                if b == 10:
                    rem, c1 = t_g_rows, c_row
                    dve.wait_ge(cum_full, 1)
                    src = ps_s[0][0:NH, :]
                    for part in range(3):
                        link(v.tensor_copy(c1, src))
                        last = v.tensor_copy(c_parts[32 * part:32 * part + NH, :], c1)
                        if part < 2:
                            link(v.tensor_tensor(rem, src, c1, ALU.subtract))
                            src = rem
                    last.then_inc(softplus_done, 1)

            def x_add(B, t, half, count, more=0, norm=None):
                dve.wait_ge(proj_full, more + (B + 1))
                if count is not None:
                    dve.wait_ge(x_added, count)
                dst = x_sb[:, t, half * 512:(half + 1) * 512]
                if norm is None:
                    v.tensor_tensor(dst, ps_proj[B % 2][:, :], dst, ALU.add).then_inc(x_added, 1)
                else:
                    v.scalar_tensor_tensor(dst, ps_proj[B % 2][:, :], xaux[:, norm, t:t + 1], dst, ALU.mult, ALU.add).then_inc(x_added, 1)

            def out_projection(B0, prep):
                prepare(prep, 1, 0)
                prepare(prep, 1, 1)
                for b in range(8):
                    split_low(B0 + b + 4)
                    if b < NT and prep == 4:
                        dve.wait_ge(x_back[b], 16)
                    x_add(B0 + b, b % 4, b // 4, None)
                    if b < 2:
                        prepare(prep, 1, b + 2)
                    if 2 <= b <= 5:
                        prepare(prep + 1, 0, b - 2)
                    if b >= 5:
                        prepare(prep + 1, 1, b - 5)
                prepare(prep + 1, 1, 3)

            def mlp(layer):
                B0, h0 = BANK_MLP[layer], 8 * CHUNKS * layer

                def hidden_low(i, j):
                    dve.wait_ge(hidh_done, i * 8 + (h0 + j + 1))
                    v.tensor_tensor(hid_l[:, j, :], p_sb[:, j % 2, :], f(hid_h[:, j, :]), ALU.subtract).then_inc(hidl_done, 1)

                def chunk(i, final):
                    for b in range(16):
                        B = B0 + b
                        if b < 8:
                            dve.wait_ge(relu_done, i * 8 + (h0 + b + 1))
                            if b >= 2:
                                dve.wait_ge(hidl_done, i * 8 + (h0 + b - 1))
                            v.scalar_tensor_tensor(p_sb[:, b % 2, :], ps_proj[B % 2][:, :], 0.0, qn[:, b % 2, :],
                                                   ALU.max, ALU.mult).then_inc(sqr_done, 1)
                        if not (final and layer == 1 and b >= 12):
                            split_low(B + 4, i * 16)
                        if 1 <= b <= 8:
                            hidden_low(i, b - 1)
                        if b >= 8:
                            x_add(B, b % 4, (b - 8) // 4, i * 8 + (X_ADDS[1 if layer == 0 else 3] + b - 8), i * 16,
                                  2 * layer + 1)
                        if final and layer == 0 and b >= 9:
                            prepare(3, 0 if b < 13 else 1, (b - 9) % NT)

                dve.wait_ge(xrs_done, 2 * layer + 2)
                with dve.Fori(0, CHUNKS - 1) as i:
                    chunk(i, False)
                chunk(CHUNKS - 1, True)
                if layer == 0:
                    prepare(3, 1, 3)

            t_g_rows = sq[0:NH, :]
            c_row = p_sb[0:NH, 1, 0:S // 2].bitcast(BF16)
            prepare(0, 0, 0)
            prepare(0, 1, 0)
            for u in range(4):
                split_low(u)
            prepare(0, 0, 1)
            prepare(0, 1, 1)
            for proj, attend in STEPS_FOX:
                step(proj, attend)
            out_projection(BANK_FOX_OUT, 1)
            v.tensor_reduce(quad[:, :], ident[:, :].rearrange("p (j r) -> p j r", r=NT), AX, ALU.add)
            v.tensor_reduce(place[:, :], ident[:, :].rearrange("p (j r) -> p r j", r=NT), AX, ALU.add).then_inc(quad_done, 1)
            mlp(0)
            for proj, attend in STEPS_DIL:
                step(proj, attend)
            out_projection(BANK_DIL_OUT, 4)
            mlp(1)

        @block.gpsimd
        def _(pool):
            g = nc.gpsimd
            own = [0]

            def link(ins):
                own[0] += 1
                ins.then_inc(pool_own, 1)
                pool.wait_ge(pool_own, own[0])

            def select(ap, pattern, base, cm, op, fill):
                link(g.affine_select(out=ap, in_=ap, compare_op=op, fill=fill, base=base, pattern=pattern, channel_multiplier=cm))

            def norm_means(norm):
                pool.wait_ge(xss_done, 4 * (norm + 1))
                link(g.tensor_scalar(xss[:, norm, :], xss[:, norm, :], 1.0 / D, EPS, ALU.mult, ALU.add))
                if norm == 2:
                    g.tensor_tensor(spread.rearrange("p (t j) -> p t j", t=NT), quad[:, :].unsqueeze(1).broadcast_to([P, NT, P // NT]),
                                    xss[:, norm, :].unsqueeze(2).broadcast_to([P, NT, P // NT]), ALU.mult).then_inc(spread_done, 1)
                if norm % 2 == 0:
                    link(g.tensor_scalar(xaux[:, norm, :], xss[:, norm, :], HD * EPS, None, ALU.mult))

            def norm_roots(norm):
                if norm == 2:
                    g.tensor_tensor(xrs[:, 4, :], xss[:, 4, :], m_half[:, 0:NT], ALU.pow)
                last = g.tensor_tensor(xrs[:, norm, :], xss[:, norm, :], m_half[:, 0:NT], ALU.pow)
                if norm % 2 == 1:
                    link(last)
                    last = g.tensor_tensor(xaux[:, norm, :], xrs[:, norm, :], xrs[:, norm, :], ALU.mult)
                last.then_inc(xrs_done, 1)

            def bank_event(s, b):
                if b >= QK_SET:
                    return
                kind, _ = SETS[s]
                n = QK_SET * s + b
                pool.wait_ge(qss_done, n + 1)
                link(g.tensor_scalar(qss[:, n % 2, :], qss[:, n % 2, :], xaux[:, norm_slot(s), b % 4:b % 4 + 1], None, ALU.add))
                g.tensor_tensor(qrs[:, n % 2, :], qss[:, n % 2, :], m_half[:, :], ALU.pow).then_inc(qrs_done, 1)
                if kind == "fox":
                    return
                pool.wait_ge(qn_done, n + 1)
                tab = 2 * kind + b // 4
                rot = qn[:, n % 2, :].rearrange("p (h d) -> p h d", d=HD)[:, :, 0:ROT]
                ta = tab_a[:, tab, b % 4, :].unsqueeze(1).broadcast_to([P, HS, ROT])
                tb = tab_b[:, tab, b % 4, :].unsqueeze(1).broadcast_to([P, HS, ROT])
                g.tensor_tensor(rt[:, 0, :, :], rot, ta, ALU.mult)
                g.tensor_tensor(rt[:, 1, :, 0:HALF], rot[:, :, HALF:ROT], tb[:, :, 0:HALF], ALU.mult)
                link(g.tensor_tensor(rt[:, 1, :, HALF:ROT], rot[:, :, 0:HALF], tb[:, :, HALF:ROT], ALU.mult))
                g.tensor_tensor(rot, rt[:, 0, :, :], rt[:, 1, :, :], ALU.add).then_inc(rope_done, 1)
                pool.wait_ge(rope_done, n - 2 * QK_SET + 1)

            merges = [0]

            def merge(s, a):
                kind, half = SETS[s]
                h, _, last_bank = ticks_of(s)[a - TICK0[s]]
                if kind not in (2, 0) or not last_bank:
                    return
                m = merges[0]
                acc = acc12[:, :, h // 2, head_cols(h)] if kind == 2 else o_sb[:, :, (HS * half + h) // 2, head_cols(h)]
                new = o_ring[:, m % 2, :, 0:VC]
                pool.wait_ge(efac_done, m + 1)
                pool.wait_ge(o_done, HS * s + h + 1)
                g.tensor_tensor(acc, acc, e_fac[:, m % 4, 0, :].unsqueeze(2).broadcast_to([P, NT, VC]), ALU.mult)
                link(g.tensor_tensor(new, new, e_fac[:, m % 4, 1, :].unsqueeze(2).broadcast_to([P, NT, VC]), ALU.mult))
                g.tensor_tensor(acc, acc, new, ALU.add).then_inc(merged, 1)
                merges[0] += 1

            def step(proj, attend):
                n = ticks_of_step(attend)
                for a in range(n):
                    if attend is not None and 3 <= a <= len(ticks_of(attend)) + 2:
                        merge(attend, TICK0[attend] + a - 3)
                    for s, b in banks_of_tick(proj, attend, a):
                        bank_event(s, b)
                        if b == 2 and s in (0, 2):
                            norm_roots(s)

            link(g.memset(ident[:, :], 0.0))
            g.affine_select(out=ident[:, :], in_=ident[:, :], compare_op=ALU.not_equal, fill=1.0, base=0,
                            pattern=[[-1, P]], channel_multiplier=1).then_inc(ident_done, 1)
            pool.wait_ge(ident_done, 1)
            link(g.memset(m_half[:, :], -0.5))
            g.memset(hg[:, :], 1.0).then_inc(consts_done, 1)
            pool.wait_ge(consts_done, 1)
            link(g.memset(causal[:, :], 0.0))
            select(causal[:, :], [[-1, P]], 0, 1, ALU.is_ge, NEG)
            link(g.memset(banded[:, :], 0.0))
            select(banded[:, 0:P], [[1, P]], 0, -1, ALU.is_ge, NEG)
            select(banded[:, P:2 * P], [[-1, P]], 0, 1, ALU.is_ge, NEG)
            link(g.memset(pick[:, :], 0.0))
            link(g.memset(c_parts[:, :], 0.0))
            for part in range(3):
                select(pick[32 * part:32 * part + NH, :], [[-1, NH]], 0, 1, ALU.not_equal, 1.0)
            for i in range(2):
                link(g.memset(v_sb[i][:, :, :, 0:VP:VP - 1], 1.0))
            link(g.memset(upto_t[:, :], -1.0))
            select(upto_t[:, :], [[1, P]], 0, -1, ALU.is_ge, 0.0)
            g.memset(ones_t[:, :], -1.0).then_inc(pool_done, 1)
            pool.wait_ge(pool_done, 1)
            norm_means(0)
            pool.wait_ge(fgain_in, 16 * 4)
            g.tensor_scalar(hg[:, 1:2], hg[:, 1:2], float(HD) ** 0.5, None, ALU.mult).then_inc(hgain_in, 1)
            step(*STEPS_FOX[0])
            pool.wait_ge(pos_in, 16 * 20)
            kg = hg[:, 2:8].rearrange("p (a b) -> p a b", b=2)[:, :, 1]
            g.tensor_scalar(kg, kg, float(HD) ** 0.5, None, ALU.mult).then_inc(hgain_in, 1)
            inv = np.float32(THETA) ** (-np.arange(HALF, dtype=np.float32) * np.float32(2.0) / np.float32(ROT))
            for j in range(HALF):
                g.memset(freq[:, j:j + 1], float(inv[j]))
            link(g.tensor_copy(pos_f[:, :], pos_i[:, :, :].rearrange("p a b -> p (a b)")))
            link(g.tensor_tensor(ang[:, :, :], pos_f[:, :].unsqueeze(2).broadcast_to([P, 2 * NT, HALF]),
                                 freq[:, :].unsqueeze(1).broadcast_to([P, 2 * NT, HALF]), ALU.mult))
            magic = float(1.5 * 2 ** 23)
            link(g.tensor_scalar(turns[:, :, :], ang[:, :, :], 1.0 / (2 * np.pi), magic, ALU.mult, ALU.add))
            link(g.tensor_scalar(turns[:, :, :], turns[:, :, :], magic, None, ALU.subtract))
            two_pi = 2 * np.pi
            c1 = 6.28125
            c2 = float(np.float32(round((two_pi - c1) * 2 ** 19) / 2 ** 19))
            c3 = float(np.float32(two_pi - c1 - c2))
            for c in (c1, c2, c3):
                link(g.tensor_scalar(sin_t[:, :, :], turns[:, :, :], c, None, ALU.mult))
                link(g.tensor_tensor(ang[:, :, :], ang[:, :, :], sin_t[:, :, :], ALU.subtract))
            pi_down = 3.1415925
            g.tensor_scalar(ang[:, :, :], ang[:, :, :], pi_down, -pi_down, ALU.min, ALU.max).then_inc(angle_done, 1)
            step(*STEPS_FOX[1])
            step(*STEPS_FOX[2])
            norm_means(1)
            norm_roots(1)
            pool.wait_ge(sin_done, 1)
            link(g.tensor_tensor(sinh_t[:, :, :], sinh_t[:, :, :], sinh_t[:, :, :], ALU.mult))
            st = sin_t[:, :, :].rearrange("p (a t) j -> p a t j", a=2)
            ch = sinh_t[:, :, :].rearrange("p (a t) j -> p a t j", a=2)
            for lay in range(2):
                for hlf in range(2):
                    c = slice(hlf * HALF, (hlf + 1) * HALF)
                    link(g.tensor_scalar(cos2[:, lay, :, c], ch[:, lay, :, :], -2.0, 1.0, ALU.mult, ALU.add))
                    link(g.tensor_scalar(sin2[:, lay, :, c], st[:, lay, :, :], 2.0 * hlf - 1.0, None, ALU.mult))
            for tab in range(6):
                lay = LAYOUT[tab // 2]
                gn = rot_g[:, tab, :]
                link(g.tensor_tensor(tab_a[:, tab, :, :], cos2[:, lay, :, :], gn.unsqueeze(1).broadcast_to([P, NT, ROT]), ALU.mult))
                for hlf in range(2):
                    c = slice(hlf * HALF, (hlf + 1) * HALF)
                    o = slice((1 - hlf) * HALF, (2 - hlf) * HALF)
                    link(g.tensor_tensor(tab_b[:, tab, :, c], sin2[:, lay, :, c], gn[:, o].unsqueeze(1).broadcast_to([P, NT, HALF]), ALU.mult))
            link(g.memset(residue[:, :], NEG))
            for d in range(0, P, NT):
                select(residue[:, :], [[-1, P]], -d, 1, ALU.not_equal, 0.0)
            pool.nop().then_inc(pool_done, 1)
            pool.wait_ge(quad_done, 1)
            norm_means(2)
            pool.wait_ge(turned_done, 1)
            pool.wait_ge(x_out, 16 * NT)
            for proj, attend in STEPS_DIL:
                step(proj, attend)
            norm_means(3)
            norm_roots(3)


_INS = ["x", "positions", "fox_norm", "fox_w_in", "fox_b_f", "fox_q_gain", "fox_k_gain", "fox_w_out",
        "dil_norm", "dil_w_in", "dil_q_gain", "dil_k_gain", "dil_w_out", "mlp_norm", "mlp_w1", "mlp_w2"]


def kernel(**inputs):
    from concourse import bacc
    from concourse.bass_utils import run_bass_kernel_spmd

    nc = bacc.Bacc("TRN2", target_bir_lowering=False, num_devices=1)
    arrays, args = {}, []
    for name in _INS:
        a = np.ascontiguousarray(inputs[name])
        arrays[f"in_{name}"] = a
        args.append(nc.dram_tensor(f"in_{name}", a.shape, mybir.dt.from_np(a.dtype), kind="ExternalInput").ap())
    args.append(nc.dram_tensor("out_0", (1, S, D), F32, kind="ExternalOutput").ap())
    trunk(nc, *args)
    r = run_bass_kernel_spmd(nc, [arrays], core_ids=[0])
    return r.results[0]["out_0"]
```
